# Optimizing a Trainium2 kernel written in Bass

```python
import jax, jax.numpy as jnp
from jax import lax
import numpy as np

D_MODEL = 1024
BATCH = 1
SEQ = 256
DEPTH = 2

N_HEADS = 16
HEAD_DIM = D_MODEL // N_HEADS
D_FF = ((8 * D_MODEL // 3 + 127) // 128) * 128
CONV_WIDTH = 3
CHUNK = 64
Q_BLOCK = 128
N_A_LAYERS = DEPTH // 2
N_B_LAYERS = DEPTH - N_A_LAYERS
RMS_EPS = 1e-6
FORGET_BIAS = 3.0


def rmsnorm(x, g):
    xf = x.astype(jnp.float32)
    y = xf * lax.rsqrt(jnp.mean(xf * xf, axis=-1, keepdims=True) + RMS_EPS)
    return (y * g.astype(jnp.float32)).astype(x.dtype)

def split_heads(t):
    b, s, _ = t.shape
    return t.reshape(b, s, N_HEADS, HEAD_DIM).transpose(0, 2, 1, 3)

def merge_heads(t):
    b, h, s, d = t.shape
    return t.transpose(0, 2, 1, 3).reshape(b, s, h * d)

def stick_breaking_attention(q, k, v):
    b, h, s, d = q.shape
    scale = HEAD_DIM ** -0.5
    n_blocks = s // Q_BLOCK
    strict = jnp.arange(Q_BLOCK)[:, None] > jnp.arange(Q_BLOCK)[None, :]
    outs = []
    for qi in range(n_blocks):
        lo, hi = qi * Q_BLOCK, (qi + 1) * Q_BLOCK
        qb = q[:, :, lo:hi].astype(jnp.float32) * scale
        kd = k[:, :, lo:hi].astype(jnp.float32)
        vd = v[:, :, lo:hi].astype(jnp.float32)
        z = jnp.einsum('bhtd,bhsd->bhts', qb, kd)
        log_keep = jnp.where(strict, jax.nn.log_sigmoid(-z), 0.0)
        later = lax.cumsum(log_keep, axis=3, reverse=True) - log_keep
        attn = jnp.where(strict, jnp.exp(jax.nn.log_sigmoid(z) + later), 0.0)
        out = jnp.einsum('bhts,bhsd->bhtd', attn, vd)
        log_surv = jnp.sum(log_keep, axis=-1)
        if qi > 0:
            kp = k[:, :, :lo].astype(jnp.float32).reshape(b, h, qi, Q_BLOCK, d)
            vp = v[:, :, :lo].astype(jnp.float32).reshape(b, h, qi, Q_BLOCK, d)
            kp = jnp.flip(jnp.moveaxis(kp, 2, 0), axis=0)
            vp = jnp.flip(jnp.moveaxis(vp, 2, 0), axis=0)

            def step(carry, kv, qb=qb):
                acc, surv = carry
                kb, vb = kv
                zb = jnp.einsum('bhtd,bhsd->bhts', qb, kb)
                lk = jax.nn.log_sigmoid(-zb)
                lat = lax.cumsum(lk, axis=3, reverse=True) - lk + surv[..., None]
                wb = jnp.exp(jax.nn.log_sigmoid(zb) + lat)
                acc = acc + jnp.einsum('bhts,bhsd->bhtd', wb, vb)
                return (acc, surv + jnp.sum(lk, axis=-1)), None

            (out, _), _ = lax.scan(step, (out, log_surv), (kp, vp))
        outs.append(out)
    return jnp.concatenate(outs, axis=2).astype(v.dtype)

def forgetting_attention(q, k, v, fcum):
    s = q.shape[2]
    scale = HEAD_DIM ** -0.5
    outs = []
    for qi in range(s // Q_BLOCK):
        lo, hi = qi * Q_BLOCK, (qi + 1) * Q_BLOCK
        qb = q[:, :, lo:hi].astype(jnp.float32) * scale
        kb = k[:, :, :hi].astype(jnp.float32)
        vb = v[:, :, :hi].astype(jnp.float32)
        logits = (jnp.einsum('bhtd,bhsd->bhts', qb, kb)
                  + fcum[:, :, lo:hi, None] - fcum[:, :, None, :hi])
        causal = (lo + jnp.arange(Q_BLOCK))[:, None] >= jnp.arange(hi)[None, :]
        p = jax.nn.softmax(jnp.where(causal, logits, -jnp.inf), axis=-1)
        outs.append(jnp.einsum('bhts,bhsd->bhtd', p, vb))
    return jnp.concatenate(outs, axis=2).astype(v.dtype)

def conv_ffn(x, w_up, conv_w, conv_b, w_down):
    hdn = x @ w_up
    hdn = lax.conv_general_dilated(
        hdn, conv_w[:, None, :], window_strides=(1,),
        padding=[(CONV_WIDTH - 1, 0)],
        dimension_numbers=('NWC', 'WIO', 'NWC'),
        feature_group_count=2 * D_FF) + conv_b
    gate, up = jnp.split(hdn, 2, axis=-1)
    return (jax.nn.gelu(gate, approximate=True) * up) @ w_down

def first_inputs(seed: int = 0) -> dict:
    key = jax.random.key(seed)
    ks = jax.random.split(key, 20)
    D, F, H = D_MODEL, D_FF, N_HEADS

    def w(k, shape, fan_in):
        return jax.random.normal(k, shape, jnp.float32) * fan_in ** -0.5

    def gain(k, shape):
        return 1.0 + 0.1 * jax.random.normal(k, shape, jnp.float32)

    return {
        "x": jax.random.normal(ks[0], (BATCH, SEQ, D), jnp.float32),
        "sb_pre_g": gain(ks[1], (N_A_LAYERS, D)),
        "sb_w_qkv": w(ks[2], (N_A_LAYERS, D, 3 * D), D),
        "sb_w_o": w(ks[3], (N_A_LAYERS, D, D), D),
        "sb_post_g": gain(ks[4], (N_A_LAYERS, D)),
        "kv_norm_g": gain(ks[5], (D,)),
        "w_kvf": w(ks[6], (D, 2 * D + H), D),
        "b_f": FORGET_BIAS + 0.5 * jax.random.normal(ks[7], (H,), jnp.float32),
        "fox_pre_g": gain(ks[8], (N_B_LAYERS, D)),
        "fox_w_q": w(ks[9], (N_B_LAYERS, D, D), D),
        "fox_w_o": w(ks[10], (N_B_LAYERS, D, D), D),
        "fox_post_g": gain(ks[11], (N_B_LAYERS, D)),
        "ffn_pre_g": gain(ks[12], (DEPTH, D)),
        "w_up": w(ks[13], (DEPTH, D, 2 * F), D),
        "conv_w": w(ks[14], (DEPTH, CONV_WIDTH, 2 * F), CONV_WIDTH),
        "conv_b": 0.02 * jax.random.normal(ks[15], (DEPTH, 2 * F), jnp.float32),
        "w_down": w(ks[16], (DEPTH, F, D), F),
        "ffn_post_g": gain(ks[17], (DEPTH, D)),
    }

def first_block(x, sb_pre_g, sb_w_qkv, sb_w_o, sb_post_g, kv_norm_g, w_kvf, b_f,
              fox_pre_g, fox_w_q, fox_w_o, fox_post_g,
              ffn_pre_g, w_up, conv_w, conv_b, w_down, ffn_post_g):
    D = D_MODEL
    h = x
    k_sh = v_sh = fcum_sh = None
    for layer in range(DEPTH):
        if layer < N_A_LAYERS:
            a = rmsnorm(h, sb_pre_g[layer])
            q, k, v = jnp.split(a @ sb_w_qkv[layer], 3, axis=-1)
            o = stick_breaking_attention(split_heads(q), split_heads(k), split_heads(v))
            h = h + rmsnorm(merge_heads(o) @ sb_w_o[layer], sb_post_g[layer])
        else:
            if layer == N_A_LAYERS:
                s_in = rmsnorm(h, kv_norm_g)
                kvf = s_in @ w_kvf
                k_sh = split_heads(kvf[..., :D])
                v_sh = split_heads(kvf[..., D:2 * D])
                log_f = jax.nn.log_sigmoid(kvf[..., 2 * D:].astype(jnp.float32)
                                           + b_f.astype(jnp.float32))
                fcum_sh = jnp.cumsum(jnp.transpose(log_f, (0, 2, 1)), axis=-1)
            j = layer - N_A_LAYERS
            a = rmsnorm(h, fox_pre_g[j])
            q = split_heads(a @ fox_w_q[j])
            o = forgetting_attention(q, k_sh, v_sh, fcum_sh)
            h = h + rmsnorm(merge_heads(o) @ fox_w_o[j], fox_post_g[j])
        f = conv_ffn(rmsnorm(h, ffn_pre_g[layer]), w_up[layer], conv_w[layer],
                     conv_b[layer], w_down[layer])
        h = h + rmsnorm(f, ffn_post_g[layer])
    return h


N_MIXERS = 2
N_ATTN_LAYERS = (DEPTH + 1) // 2
N_REC_LAYERS = DEPTH // 2

HEAD_DIM_2 = 64
N_HEADS_2 = D_MODEL // HEAD_DIM_2
N_KV_HEADS = 2
GROUP = N_HEADS_2 // N_KV_HEADS
ATTN_WIDTH = N_HEADS_2 * HEAD_DIM_2
KV_WIDTH = N_KV_HEADS * HEAD_DIM_2
ATTN_IN = 2 * ATTN_WIDTH + 2 * KV_WIDTH
WINDOW = 128
ATTN_BLOCK = 128
ROPE_THETA = 500000.0
ROPE_DIM = HEAD_DIM_2 // 4

REC_HEADS = 8
REC_KEY_DIM = 128
REC_VALUE_DIM = D_MODEL // REC_HEADS
FORGET_DIM = REC_HEADS * REC_KEY_DIM
REC_WIDTH = REC_HEADS * REC_VALUE_DIM
REC_IN = 2 * FORGET_DIM + 2 * REC_WIDTH
REC_CHUNK = 32

NORM_EPS = 1e-6


def rmsnorm_2(x, w):
    xf = x.astype(jnp.float32)
    y = xf * lax.rsqrt(jnp.mean(xf * xf, axis=-1, keepdims=True) + NORM_EPS)
    return (y * w.astype(jnp.float32)).astype(x.dtype)

def partial_rope(x, positions):
    half = ROPE_DIM // 2
    inv_freq = ROPE_THETA ** (-(jnp.arange(half, dtype=jnp.float32) * 2.0 / ROPE_DIM))
    ang = positions.astype(jnp.float32)[..., None] * inv_freq
    cos = jnp.cos(ang)[:, :, None, :]
    sin = jnp.sin(ang)[:, :, None, :]
    x1 = x[..., :half].astype(jnp.float32)
    x2 = x[..., half:ROPE_DIM].astype(jnp.float32)
    r1 = x1 * cos - x2 * sin
    r2 = x2 * cos + x1 * sin
    return jnp.concatenate([r1.astype(x.dtype), r2.astype(x.dtype), x[..., ROPE_DIM:]], axis=-1)

def sliding_window_gqa(q, k, v, sinks):
    B, T = q.shape[0], q.shape[1]
    nb = T // ATTN_BLOCK
    qb = q.reshape(B, nb, ATTN_BLOCK, N_KV_HEADS, GROUP, HEAD_DIM_2).transpose(1, 0, 2, 3, 4, 5)

    def span(t):
        tb = t.reshape(B, nb, ATTN_BLOCK, N_KV_HEADS, HEAD_DIM_2)
        prev = jnp.pad(tb, ((0, 0), (1, 0), (0, 0), (0, 0), (0, 0)))[:, :-1]
        return jnp.concatenate([prev, tb], axis=2).transpose(1, 0, 2, 3, 4)

    kk, vv = span(k), span(v)
    q_rel = jnp.arange(ATTN_BLOCK)[:, None] + ATTN_BLOCK
    k_rel = jnp.arange(2 * ATTN_BLOCK)[None, :]
    band = (k_rel <= q_rel) & (q_rel - k_rel < WINDOW)
    sink = sinks.astype(jnp.float32).reshape(N_KV_HEADS, GROUP)[None, :, :, None]
    scale = HEAD_DIM_2 ** -0.5

    def block(args):
        qi, ki, vi, idx = args
        s = jnp.einsum('bqhgd,bkhd->bhgqk', qi, ki, preferred_element_type=jnp.float32) * scale
        valid = band & ((idx > 0) | (k_rel >= ATTN_BLOCK))
        s = jnp.where(valid, s, -jnp.inf)
        m = jnp.maximum(jnp.max(s, axis=-1), sink)
        p = jnp.exp(s - m[..., None])
        denom = jnp.sum(p, axis=-1) + jnp.exp(sink - m)
        p = (p / denom[..., None]).astype(vi.dtype)
        return jnp.einsum('bhgqk,bkhd->bqhgd', p, vi)

    out = lax.map(block, (qb, kk, vv, jnp.arange(nb)))
    return out.transpose(1, 0, 2, 3, 4, 5).reshape(B, T, ATTN_WIDTH)

def attention_mixer(h, positions, w_in, b_in, sinks, w_out, b_out):
    B, T = h.shape[0], h.shape[1]
    proj = h @ w_in + b_in
    q, k, v, z = jnp.split(proj, [ATTN_WIDTH, ATTN_WIDTH + KV_WIDTH, ATTN_WIDTH + 2 * KV_WIDTH], axis=-1)
    q = partial_rope(q.reshape(B, T, N_HEADS_2, HEAD_DIM_2), positions)
    k = partial_rope(k.reshape(B, T, N_KV_HEADS, HEAD_DIM_2), positions)
    v = v.reshape(B, T, N_KV_HEADS, HEAD_DIM_2)
    o = sliding_window_gqa(q, k, v, sinks)
    return (o * jax.nn.silu(z)) @ w_out + b_out

def chunked_gated_recurrence(q, k, v, log_f):
    B, T, H, K = q.shape
    V = v.shape[-1]
    nc = T // REC_CHUNK

    def to_chunks(t):
        return t.reshape(B, nc, REC_CHUNK, H, t.shape[-1]).transpose(1, 0, 3, 2, 4)

    qc, kc, vc, gc = to_chunks(q), to_chunks(k), to_chunks(v), to_chunks(log_f)
    causal = jnp.tril(jnp.ones((REC_CHUNK, REC_CHUNK), dtype=bool))[:, :, None]

    def step(S, inp):
        qi, ki, vi, gi = inp
        b = jnp.cumsum(gi, axis=2)
        b_last = b[:, :, -1:, :]
        o_inter = jnp.einsum('bhck,bhkv->bhcv', qi * jnp.exp(b), S)
        diff = b[:, :, :, None, :] - b[:, :, None, :, :]
        decay = jnp.exp(jnp.where(causal, diff, -jnp.inf))
        scores = jnp.einsum('bhtk,bhtsk->bhts', qi, decay * ki[:, :, None, :, :])
        o_intra = jnp.einsum('bhts,bhsv->bhtv', scores, vi)
        S_new = S * jnp.exp(b_last)[:, :, 0, :, None] + jnp.einsum(
            'bhck,bhcv->bhkv', ki * jnp.exp(b_last - b), vi)
        return S_new, o_inter + o_intra

    S0 = jnp.zeros((B, H, K, V), jnp.float32)
    _, o = lax.scan(step, S0, (qc, kc, vc, gc))
    return o.transpose(1, 0, 3, 2, 4).reshape(B, T, H, V)

def hgrn2_mixer(h, lower_bound, w_in, gnorm_w, w_out):
    B, T = h.shape[0], h.shape[1]
    proj = h @ w_in
    q, f, i, z = jnp.split(proj, [FORGET_DIM, 2 * FORGET_DIM, 2 * FORGET_DIM + REC_WIDTH], axis=-1)
    q = jax.nn.silu(q.astype(jnp.float32)).reshape(B, T, REC_HEADS, REC_KEY_DIM)
    lb = lower_bound.astype(jnp.float32)
    log_f = jnp.logaddexp(jnp.log(lb), jnp.log1p(-lb) + jax.nn.log_sigmoid(f.astype(jnp.float32)))
    k = -jnp.expm1(log_f)
    log_f = log_f.reshape(B, T, REC_HEADS, REC_KEY_DIM)
    k = k.reshape(B, T, REC_HEADS, REC_KEY_DIM)
    v = i.astype(jnp.float32).reshape(B, T, REC_HEADS, REC_VALUE_DIM)
    o = chunked_gated_recurrence(q, k, v, log_f)
    o = o * lax.rsqrt(jnp.mean(o * o, axis=-1, keepdims=True) + NORM_EPS) * gnorm_w.astype(jnp.float32)
    o = o.reshape(B, T, REC_WIDTH) * jax.nn.silu(z.astype(jnp.float32))
    return o.astype(h.dtype) @ w_out

def second_inputs(seed: int = 0) -> dict:
    key = jax.random.key(seed)
    ks = jax.random.split(key, 16)
    f32 = jnp.float32
    x = jax.random.normal(ks[0], (BATCH, SEQ, D_MODEL), f32)
    offsets = jax.random.randint(ks[1], (BATCH, 1), 0, 4096, dtype=jnp.int32)
    positions = offsets + jnp.arange(SEQ, dtype=jnp.int32)[None, :]
    pre_norm_w = 1.0 + 0.02 * jax.random.normal(ks[2], (DEPTH, D_MODEL), f32)
    post_norm_w = 1.0 + 0.02 * jax.random.normal(ks[3], (DEPTH, D_MODEL), f32)
    attn_w_in = jax.random.normal(ks[4], (N_ATTN_LAYERS, D_MODEL, ATTN_IN), f32) * D_MODEL ** -0.5
    attn_b_in = 0.02 * jax.random.normal(ks[5], (N_ATTN_LAYERS, ATTN_IN), f32)
    attn_sinks = 0.5 * jax.random.normal(ks[6], (N_ATTN_LAYERS, N_HEADS_2), f32)
    attn_w_out = jax.random.normal(ks[7], (N_ATTN_LAYERS, ATTN_WIDTH, D_MODEL), f32) * ATTN_WIDTH ** -0.5
    attn_b_out = 0.02 * jax.random.normal(ks[8], (N_ATTN_LAYERS, D_MODEL), f32)
    rec_w_in = jax.random.normal(ks[9], (N_REC_LAYERS, D_MODEL, REC_IN), f32) * D_MODEL ** -0.5
    rec_lb_logits = 0.5 * jax.random.normal(ks[10], (DEPTH, FORGET_DIM), f32)
    rec_gnorm_w = 1.0 + 0.02 * jax.random.normal(ks[11], (N_REC_LAYERS, REC_VALUE_DIM), f32)
    rec_w_out = jax.random.normal(ks[12], (N_REC_LAYERS, REC_WIDTH, D_MODEL), f32) * REC_WIDTH ** -0.5
    return {"x": x, "positions": positions, "pre_norm_w": pre_norm_w, "post_norm_w": post_norm_w,
            "attn_w_in": attn_w_in, "attn_b_in": attn_b_in, "attn_sinks": attn_sinks,
            "attn_w_out": attn_w_out, "attn_b_out": attn_b_out, "rec_w_in": rec_w_in,
            "rec_lb_logits": rec_lb_logits, "rec_gnorm_w": rec_gnorm_w, "rec_w_out": rec_w_out}

def second_block(x, positions, pre_norm_w, post_norm_w, attn_w_in, attn_b_in, attn_sinks,
              attn_w_out, attn_b_out, rec_w_in, rec_lb_logits, rec_gnorm_w, rec_w_out):
    probs = jax.nn.softmax(rec_lb_logits.astype(jnp.float32), axis=0)
    cum = jnp.cumsum(probs, axis=0)
    lower_bounds = cum - cum[0:1]
    for layer in range(DEPTH):
        h = rmsnorm_2(x, pre_norm_w[layer])
        j = layer // N_MIXERS
        if layer % N_MIXERS == 0:
            y = attention_mixer(h, positions, attn_w_in[j], attn_b_in[j], attn_sinks[j],
                                attn_w_out[j], attn_b_out[j])
        else:
            y = hgrn2_mixer(h, lower_bounds[layer], rec_w_in[j], rec_gnorm_w[j], rec_w_out[j])
        x = x + rmsnorm_2(y, post_norm_w[layer])
    return x


def setup_inputs(seed=0):
    out = dict(first_inputs(seed))
    for name, value in second_inputs(seed + 1).items():
        if name != "x":
            out[name + "_2"] = value
    return out


def reference(
    x, sb_pre_g, sb_w_qkv, sb_w_o, sb_post_g, kv_norm_g, w_kvf, b_f, fox_pre_g, fox_w_q,
    fox_w_o, fox_post_g, ffn_pre_g, w_up, conv_w, conv_b, w_down, ffn_post_g, positions_2,
    pre_norm_w_2, post_norm_w_2, attn_w_in_2, attn_b_in_2, attn_sinks_2, attn_w_out_2,
    attn_b_out_2, rec_w_in_2, rec_lb_logits_2, rec_gnorm_w_2, rec_w_out_2,
):
    x = first_block(
        x, sb_pre_g, sb_w_qkv, sb_w_o, sb_post_g, kv_norm_g, w_kvf, b_f, fox_pre_g, fox_w_q,
        fox_w_o, fox_post_g, ffn_pre_g, w_up, conv_w, conv_b, w_down, ffn_post_g,
    )
    return second_block(
        x, positions_2, pre_norm_w_2, post_norm_w_2, attn_w_in_2, attn_b_in_2, attn_sinks_2,
        attn_w_out_2, attn_b_out_2, rec_w_in_2, rec_lb_logits_2, rec_gnorm_w_2, rec_w_out_2,
    )


_drawn_inputs = setup_inputs


def setup_inputs(seed=0):
    import zlib

    import numpy as np

    out = dict(_drawn_inputs(seed))
    spreads = {}
    factors = {'pre_norm_w_2': 3.141,
     'post_norm_w_2': 4.831,
     'attn_sinks_2': 5.254,
     'rec_lb_logits_2': 2.802,
     'rec_gnorm_w_2': 27.207,
     'attn_b_out_2': 8.0}
    for name, (base, spread) in spreads.items():
        noise = np.random.default_rng([zlib.crc32(name.encode()), seed]).standard_normal(out[name].shape)
        drawn = base * np.exp(spread * noise) if base else spread * noise
        out[name] = __import__('jax').numpy.asarray(drawn.astype(out[name].dtype))
    for name, factor in factors.items():
        out[name] = (out[name] * factor).astype(out[name].dtype)
    return out
```

```python
from contextlib import ExitStack

import numpy as np
import concourse.bass as bass
from concourse import mybir

F32 = mybir.dt.float32
F32R = mybir.dt.float32r
BF16 = mybir.dt.bfloat16
I32 = mybir.dt.int32
I8 = mybir.dt.int8
ALU = mybir.AluOpType
ACT = mybir.ActivationFunctionType
AX = mybir.AxisListType

P = 128
D = 1024
T = 256
TT = T // P
KT = D // P
H = 16
DH = D // H
FF = 2816
NJ = FF // 256
KVW = 128
REC_H = 8
EPS = 1e-6
QSCALE = DH ** -0.5
NEG = -1e30
ROPE_HALF = 8
ROPE_THETA = 500000.0
UNIT = 2048
RAW = 3
HL = 3

PLAN = [("sb_qk", "T", 4), ("sb_v", "tok", 2), ("sb_o", "o", 2), ("ffn0", "ffn", NJ),
        ("fox_k", "T", 2), ("fox_v", "tok", 2), ("fox_q", "T", 2), ("fox_o", "o", 2), ("ffn1", "ffn", NJ),
        ("at_q", "tok", 2), ("at_kv", "narrow", 1), ("at_z", "T", 2), ("at_o", "o", 2),
        ("rec_f", "T", 2), ("rec_q", "T", 2), ("rec_z", "tok", 2), ("rec_i", "tok", 2), ("rec_o", "o", 2)]
UNITS_OF = {"T": 2, "tok": 2, "narrow": 1, "o": 2, "ffn": 3}
BY = {"at_q": "V", "at_kv": "V", "at_z": "S", "ffn0": "V", "ffn1": "V"}

U0, E0 = {}, {}
V_FREED, S_FREED = [], []
_u = _v = _s = 0
for _name, _kind, _n in PLAN:
    U0[_name], E0[_name] = _u, len(V_FREED)
    _u += UNITS_OF[_kind] * _n
    if _kind != "o":
        for _c in range(_n):
            _v += "V" in BY.get(_name, "VS")
            _s += "S" in BY.get(_name, "VS")
            V_FREED.append(_v)
            S_FREED.append(_s)
NU = _u

PV = {}
_c = 0
for _name, _n in [("sb_pre", 8), ("kv", 8), ("fox_pre", 8), ("ffn_pre0", 8), ("ffn_pre1", 8), ("at_pre", 8),
                  ("rec_pre", 8), ("bz", 8), ("lb0", 8), ("lb1", 8), ("conv", 2 * 22 * 2 * 4)]:
    PV[_name] = _c
    _c += _n
NPV = _c


def build(nc, stream, pvec, post_g, x_in, wf, bf, b_in, b_out, sinks, gnorm, pos, out):
    with ExitStack() as ctx:
        def sb(name, shape, dt=F32):
            return ctx.enter_context(nc.sbuf_tensor(name, shape, dt))

        def sem(name):
            return ctx.enter_context(nc.semaphore(name))

        raw = sb("raw", [P, RAW, UNIT])
        w_hi = sb("w_hi", [P, HL, UNIT], F32R)
        w_lo = sb("w_lo", [P, HL, UNIT], F32R)
        xT_hi = sb("xT_hi", [P, KT, T], F32R)
        xT_lo = sb("xT_lo", [P, KT, T], F32R)
        oT_hi = sb("oT_hi", [P, KT, T], F32R)
        oT_lo = sb("oT_lo", [P, KT, T], F32R)
        h = sb("h", [P, TT, D])
        hn = sb("hn", [P, TT, D])
        qT = sb("qT", [P, KT, T])
        kT = sb("kT", [P, KT, T])
        vt = sb("vt", [P, TT, D])
        gbc = sb("gbc", [P, D])
        pv = sb("pv", [P, NPV])
        arena = sb("arena", [P, 11264])
        ident = sb("ident", [P, P])
        ident_b = sb("ident_b", [P, P], BF16)
        neg_tri = sb("neg_tri", [P, P])
        neg_ones = sb("neg_ones", [P, P])
        mask_stick = sb("mask_stick", [P, 384], BF16)
        mask_causal = sb("mask_causal", [P, 384], BF16)
        mask_window = sb("mask_window", [P, 384], BF16)
        mask_level = sb("mask_level", [P, 8, P], I8)
        wf_sb = sb("wf_sb", [P, KT, H])
        bf_sb = sb("bf_sb", [H, 1])
        neg_f = sb("neg_f", [H, T])
        ftmp = sb("ftmp", [H, 3, T])
        ones_row = sb("ones_row", [P, T])
        sink_bc = sb("sink_bc", [P, H])
        gn_bc = sb("gn_bc", [P, P])
        pos_i = sb("pos_i", [P, TT], I32)
        pos_f = sb("pos_f", [P, TT])
        ang = sb("ang", [P, 4, TT, ROPE_HALF])
        cosin = sb("cosin", [P, 2, TT, ROPE_HALF])
        eps_t = sb("eps_t", [P, 1])
        st = sb("st", [P, 12, 6, TT])
        nmx = sb("nmx", [P, 2, H, 2])
        mx = sb("mx", [P, 2, H, 2])
        sums = sb("sums", [P, 2, H, 2])
        esink = sb("esink", [P, H, 2])
        rsum = sb("rsum", [P, 2, H, 2])
        lbv = sb("lbv", [P, 5, KT])
        rst = sb("rst", [P, 6, TT * REC_H])

        psC = ctx.enter_context(nc.psum_tensor("psC", [P, 4, 512], F32))
        psD = ctx.enter_context(nc.psum_tensor("psD", [P, 4, 512], F32))
        psD_rows = psD[:, :, :].rearrange("p (t b) n -> p t (b n)", t=TT)

        raw_loaded = [sem(f"raw_loaded{i}") for i in range(RAW)]
        hi_done = sem("hi_done")
        lo_done = sem("lo_done")
        unit_done = sem("unit_done")
        chunk_freed_v = sem("chunk_freed_v")
        chunk_freed_s = sem("chunk_freed_s")
        x_loaded = sem("x_loaded")
        small_loaded = sem("small_loaded")
        gbc_loaded = sem("gbc_loaded")
        bias_loaded = sem("bias_loaded")
        consts_pool = sem("consts_pool")
        consts_dve = sem("consts_dve")
        act_step = sem("act_step")
        dve_step = sem("dve_step")
        pool_step = sem("pool_step")
        norm_ss = sem("norm_ss")
        norm_guess = sem("norm_guess")
        norm_scaled = sem("norm_scaled")
        xT_turned = sem("xT_turned")
        xT_hi_done = sem("xT_hi_done")
        xT_lo_done = sem("xT_lo_done")
        h_new = sem("h_new")
        ysum = sem("ysum")
        sz = {n: sem(f"stick_{n}") for n in ("logit", "abs", "exp", "ln", "keep", "later", "prob", "out", "ohi", "olo")}
        sm = [{n: sem(f"{s}_{n}") for n in ("logit", "max", "exp", "norm", "turned", "pT", "out", "gated", "ohi", "olo")}
              for s in ("fox", "win")]
        forget = {n: sem(f"forget_{n}") for n in ("product", "bias", "exp", "ln", "cum")}
        rope = {n: sem(f"rope_{n}") for n in ("arg", "sin", "applied", "q_turned", "q_copied", "k_turned", "k_copied")}
        ffn = [{n: sem(f"ffn{i}_{n}") for n in ("centre", "tap1", "gate", "gelu", "g", "g_split")} for i in range(2)]
        rec = {n: sem(f"rec_{n}") for n in ("v1", "s1", "silu", "ready", "kdiff", "qdiff", "lexp", "kx", "qx", "level",
                                            "picked", "o", "osq", "oss", "oguess", "gated", "turned", "ohi", "olo")}
        stored = sem("stored")

        block = ctx.enter_context(nc.Block())

        def region(at, n):
            return arena[:, at:at + n]

        st_abs = [region(384 * i, 384) for i in range(2)]
        st_exp = [region(768 + 384 * i, 384) for i in range(2)]
        st_keep = [region(1536 + 384 * i, 384) for i in range(3)]
        st_prob = [region(2688 + 384 * i, 384) for i in range(3)]
        sm_p = [region(384 * i, 384) for i in range(3)]
        sm_pT = [region(1152 + 384 * i, 384) for i in range(3)]
        sel = arena[0:H, 5632:7680].rearrange("p (h n) -> p h n", h=H)
        cv = region(0, 2048).rearrange("p (b g a t) -> p b g a t", b=2, g=2, a=2)
        ge = region(2048, 1024).rearrange("p (b n) -> p b n", b=2)
        gf = region(3072, 512).rearrange("p (a t) -> p a t", a=2)
        qk_tok = region(2304, 2304).rearrange("p (t w) -> p t w", t=TT)
        kdup = region(4608, 512).rearrange("p (t g r d) -> p t g r d", t=TT, g=2, r=2)
        rtmp = region(5120, 1152).rearrange("p (i n d) -> p i n d", i=4, d=ROPE_HALF)
        bin_bc = region(6272, 1280)
        bout_bc = region(7552, 1024)
        ysb = region(8576, 2048).rearrange("p (t n) -> p t n", t=TT)
        gated_t = region(10624, 512).rearrange("p (b n) -> p b n", b=2)
        cum = region(0, 2048)
        kk = region(2048, 2048)
        X = [region(4096, 2048), region(6144, 2048)]
        sc_diag = region(8192, 2048)
        sc_cross = region(10240, 1024)
        LV = kT[:, :, :].rearrange("p k t -> p (k t)")
        zT = hn[:, :, :].rearrange("p t (k n) -> p (t k) n", n=T)
        gT_hi = oT_hi[:, 0:4, :].rearrange("p (b a) t -> p b a t", b=2)
        gT_lo = oT_lo[:, 0:4, :].rearrange("p (b a) t -> p b a t", b=2)

        def col(name, i=0, n=1):
            return pv[:, PV[name] + i:PV[name] + i + n]

        def bank(e, b):
            return psC[:, 2 * (e % 2) + b, :]

        def unit_hi(u):
            return w_hi[:, u % HL, :]

        def unit_lo(u):
            return w_lo[:, u % HL, :]

        def level_view(ap, m):
            return ap.rearrange("p (b two m) -> p b two m", two=2, m=m)

        def bc(ap2, n):
            return ap2.unsqueeze(2).to_broadcast([ap2.shape[0], ap2.shape[1], n])

        PRE = {"sb": 0, "ffn0": 1, "fox": 2, "ffn1": 3, "at": 4, "rec": 5}
        LEVELS = [64, 32, 16, 8, 4, 2, 1]

        @block.sync
        def _(sp):
            for u in range(RAW):
                sp.dma_start(raw[:, u, :], stream[u]).then_inc(raw_loaded[u], 16)

            def load(u, slot):
                sp.wait_ge(lo_done, u - RAW + 1)
                sp.dma_start(raw[:, slot, :], stream[u]).then_inc(raw_loaded[slot], 16)

            whole = NU // RAW
            with sp.Fori(1, whole) as i:
                for s in range(RAW):
                    load(i * RAW + s, s)
            for u in range(whole * RAW, NU):
                load(u, u % RAW)
            sp.wait_ge(h_new, 6 * TT)
            sp.dma_start(out.rearrange("b (t p) d -> p (b t) d", p=P), h[:, :, :]).then_inc(stored, 16)
            sp.wait_ge(stored, 16)

        @block.gpsimd
        def _(pool):
            pool.dma_start(h[:, :, :], x_in.rearrange("b (t p) d -> p (b t) d", p=P)).then_inc(x_loaded, 16)
            for dst, src in ((pv[:, :], pvec), (wf_sb[:, :, :], wf), (bf_sb[:, :], bf), (pos_i[:, :], pos),
                             (sink_bc[:, :], sinks.partition_broadcast(P)), (gn_bc[:, :], gnorm.partition_broadcast(P))):
                pool.dma_start(dst, src).then_inc(small_loaded, 16)
            pool.dma_start(gbc[:, :], post_g[0].partition_broadcast(P)).then_inc(gbc_loaded, 16)

            fills = [(ident, 0.0), (ident_b, 0.0), (neg_tri, -1.0), (neg_ones, -1.0), (mask_stick, 0.0),
                     (mask_causal, 0.0), (mask_window, 0.0)]
            for t, value in fills:
                nc.gpsimd.memset(t[:, :], value).then_inc(pool_step, 1)
            nc.gpsimd.memset(sel, 0.0).then_inc(pool_step, 1)
            nc.gpsimd.memset(mask_level[:, :, :], 0).then_inc(pool_step, 1)
            done = len(fills) + 2
            pool.wait_ge(pool_step, done)
            for li, m in enumerate(LEVELS):
                half = level_view(mask_level[:, li + 1, :], m)[:, :, 1, :]
                nc.gpsimd.memset(half, 1).then_inc(pool_step, 1)
                done += 1
            pool.wait_ge(pool_step, done)

            def keep(view, op, fill, base, pattern, mult):
                return nc.gpsimd.affine_select(out=view, in_=view, compare_op=op, fill=fill, base=base,
                                               pattern=pattern, channel_multiplier=mult)

            for t in (ident, ident_b):
                keep(t[:, :], ALU.not_equal, 1.0, 0, [[-1, P]], 1).then_inc(consts_pool, 1)
            keep(mask_level[:, 0, :], ALU.not_equal, 1.0, 0, [[-1, P]], 1).then_inc(consts_pool, 1)
            keep(neg_tri[:, :], ALU.is_ge, 0.0, 0, [[-1, P]], 1).then_inc(consts_pool, 1)
            for a in (0, 256):
                keep(mask_stick[:, a:a + P], ALU.is_gt, NEG, 0, [[1, P]], -1).then_inc(consts_pool, 1)
                keep(mask_causal[:, a:a + P], ALU.is_ge, NEG, 0, [[-1, P]], 1).then_inc(consts_pool, 1)
                keep(mask_window[:, a:a + P], ALU.is_ge, NEG, 0, [[-1, P]], 1).then_inc(consts_pool, 1)
            keep(mask_window[:, P:2 * P], ALU.is_gt, NEG, 0, [[1, P]], -1).then_inc(consts_pool, 1)
            keep(sel, ALU.not_equal, 1.0, 0, [[-1, H], [0, P]], 1).then_inc(consts_pool, 1)
            for li, m in enumerate(LEVELS):
                half = level_view(mask_level[:, li + 1, :], m)[:, :, 1, :]
                keep(half, ALU.is_ge, 0.0, 0, [[-2 * m, P // (2 * m)], [0, m]], 1).then_inc(pool_step, 1)
                done += 1
            pool.wait_ge(pool_step, done)
            for li, m in enumerate(LEVELS):
                half = level_view(mask_level[:, li + 1, :], m)[:, :, 1, :]
                keep(half, ALU.is_ge, 0.0, m - 1, [[2 * m, P // (2 * m)], [0, m]], -1).then_inc(consts_pool, 1)

            def next_gain(i):
                pool.wait_ge(h_new, TT * i)
                pool.dma_start(gbc[:, :], post_g[i].partition_broadcast(P)).then_inc(gbc_loaded, 16)

            def gate_parts(layer):
                f, u0 = ffn[layer], U0[f"ffn{layer}"]

                def split(d, par, peeled):
                    pool.wait_ge(f["g"], d + 1)
                    if not peeled or d >= 2:
                        pool.wait_ge(unit_done, u0 + 3 * d - 1)
                    hi, lo = gT_hi[:, par], gT_lo[:, par]
                    one = ones_row[:, :].unsqueeze(1).to_broadcast([P, 2, T])
                    nc.gpsimd.tensor_tensor(hi, gf, one, ALU.mult).then_inc(f["g_split"], 1)
                    pool.wait_ge(f["g_split"], 2 * d + 1)
                    nc.gpsimd.tensor_tensor(lo, gf, hi.bitcast(F32), ALU.subtract).then_inc(f["g_split"], 1)

                for d in range(3):
                    split(d, d % 2, True)
                with pool.Fori(0, (NJ - 3) // 2) as i:
                    for par in range(2):
                        split(2 * i + (3 + par), (3 + par) % 2, False)

            next_gain(1)
            gate_parts(0)
            next_gain(2)
            next_gain(3)
            gate_parts(1)
            next_gain(4)
            pool.dma_start(bin_bc, b_in.partition_broadcast(P)).then_inc(bias_loaded, 16)
            pool.dma_start(bout_bc, b_out.partition_broadcast(P)).then_inc(bias_loaded, 16)
            next_gain(5)

            pool.wait_ge(rec["ready"], 1)
            for li, m in enumerate(LEVELS):
                c4, l4, x4, k4 = (level_view(a, m) for a in (cum, LV, X[li % 2], kk))
                nb = T * REC_H // (2 * m)
                ref = c4[:, :, 0, m - 1:m].to_broadcast([P, nb, m])
                if li >= 1:
                    pool.wait_ge(rec["kx"], li)
                    pool.wait_ge(rec["qx"], li)
                nc.gpsimd.tensor_tensor(l4[:, :, 0, :], ref, c4[:, :, 0, :], ALU.subtract).then_inc(rec["kdiff"], 1)
                pool.wait_ge(rec["lexp"], li + 1)
                if li >= 2:
                    pool.wait_ge(rec["level"], 2 * (li - 2) + 4)
                nc.gpsimd.tensor_tensor(x4[:, :, 0, :], l4[:, :, 0, :], k4[:, :, 0, :], ALU.mult).then_inc(rec["kx"], 1)

        @block.scalar
        def _(act):
            steps = [0]

            def settle(ins):
                ins.then_inc(act_step, 1)
                steps[0] += 1
                act.wait_ge(act_step, steps[0])

            nsplit = [0]

            def split_hi(u, slot, raw_slot, loads, peeled):
                act.wait_ge(raw_loaded[raw_slot], 16 * loads)
                if not peeled or u >= HL:
                    act.wait_ge(unit_done, u - HL + 1)
                nc.scalar.activation(w_hi[:, slot, :], raw[:, raw_slot, :], ACT.Copy).then_inc(hi_done, 1)

            def split_to(n):
                for u in range(nsplit[0], min(n, NU)):
                    split_hi(u, u % HL, u % RAW, u // RAW + 1, True)
                nsplit[0] = max(nsplit[0], min(n, NU))

            def rows_guess(n, tt, src, junk):
                nc.scalar.activation(junk, src, ACT.Square, accum_out=st[:, n, 0, tt:tt + 1]).then_inc(norm_ss, 1)
                act.wait_ge(norm_ss, TT * n + tt + 1)
                settle(nc.scalar.activation(st[:, n, 1, tt:tt + 1], st[:, n, 0, tt:tt + 1], ACT.Ln,
                                            bias=eps_t[:, :], scale=1.0 / D))
                nc.scalar.activation(st[:, n, 2, tt:tt + 1], st[:, n, 1, tt:tt + 1], ACT.Exp, scale=-0.5).then_inc(norm_guess, 1)

            def junk(tt):
                return kT[:, 4 * tt:4 * tt + 4, :].rearrange("p k t -> p (k t)")

            def pre(n, gains):
                for tt in range(TT):
                    act.wait_ge(h_new, TT * n) if n else act.wait_ge(x_loaded, 16)
                    rows_guess(2 * n, tt, h[:, tt, :], junk(tt))
                for gi, (gain, hi) in enumerate(gains):
                    for b in range(4):
                        act.wait_ge(xT_turned, KT * TT * n + KT + 2 * b + 2)
                        if gi:
                            act.wait_ge(xT_lo_done, xt_base(n) + 4 * gi)
                        for k in (2 * b, 2 * b + 1):
                            ins = nc.scalar.activation(hi[:, k, :], psD[:, b, (k % 2) * T:(k % 2) * T + T], ACT.Copy,
                                                       scale=col(gain, k))
                        ins.then_inc(xT_hi_done, 1)

            def post(i):
                for tt in range(TT):
                    if i == 4:
                        act.wait_ge(ysum, tt + 1)
                        src = ysb[:, tt, :]
                    else:
                        act.wait_ge(unit_done, U0_END[i])
                        src = psD_rows[:, tt, :]
                    rows_guess(2 * i + 1, tt, src, junk(tt))

            def chunk_wait(name, c):
                act.wait_ge(unit_done, U0[name] + 2 * c + 2)

            def evac(name, c, dst, **kw):
                chunk_wait(name, c)
                nc.scalar.activation(dst, bank(E0[name] + c, 1), ACT.Copy, **kw).then_inc(chunk_freed_s, 1)

            def feature_half(dst, c):
                return dst[:, 4 * c + 2:4 * c + 4, :].rearrange("p k t -> p (k t)")

            def conv_ffn(layer):
                f, u0, e0 = ffn[layer], U0[f"ffn{layer}"], E0[f"ffn{layer}"]

                def centre(j, par, e, peeled):
                    act.wait_ge(unit_done, u0 + 3 * j + (1 if not peeled or j else 2))
                    if not peeled or j >= 2:
                        act.wait_ge(f["g"], j - 1)
                    for g in range(2):
                        for a in range(2):
                            at = PV["conv"] + layer * 176 + (2 * j + a) * 8 + g * 4
                            ins = nc.scalar.activation(cv[:, par, g, a, :], psC[:, 2 * (e % 2) + g, a * T:a * T + T], ACT.Identity,
                                                       scale=pv[:, bass.ds(at + 2, 1)], bias=pv[:, bass.ds(at + 3, 1)])
                        ins.then_inc(f["centre"], 1)

                def gelu(j, par):
                    act.wait_ge(f["gate"], j + 1)
                    nc.scalar.activation(ge[:, par, :], cv[:, par, 0, :, :].rearrange("p a t -> p (a t)"),
                                         ACT.Gelu_apprx_tanh).then_inc(f["gelu"], 1)

                for j in range(3):
                    split_to(u0 + 3 * j + 3)
                    centre(j, j % 2, e0 + j, True)
                    split_to(u0 + 3 * j + 4)
                    gelu(j, j % 2)
                with act.Fori(0, (NJ - 3) // 2) as i:
                    for par in range(2):
                        j = 2 * i + (3 + par)

                        def split(k):
                            first = u0 + 3 * (3 + par) + k
                            split_hi(first + 6 * i, first % HL, first % RAW, i * (6 // RAW) + (first // RAW + 1), False)

                        split(1)
                        split(2)
                        centre(j, (3 + par) % 2, e0 + 3 + par, False)
                        split(3)
                        gelu(j, (3 + par) % 2)
                nsplit[0] = u0 + 3 * NJ + 1

            def out_parts(s, p, src, dst_sem):
                nc.scalar.activation(oT_hi[:, p, :], src, ACT.Copy).then_inc(dst_sem, 1)

            def stick():
                s = sz
                for i in range(H + 5):
                    if i < H:
                        act.wait_ge(s["abs"], i + 1)
                        if i >= 2:
                            act.wait_ge(s["keep"], i - 1)
                        nc.scalar.activation(st_exp[i % 2], st_abs[i % 2], ACT.Exp, scale=-1.0).then_inc(s["exp"], 1)
                    if 0 <= i - 2 < H:
                        j = i - 2
                        act.wait_ge(s["later"], j + 1)
                        if j >= 3:
                            act.wait_ge(s["out"], j - 2)
                        nc.scalar.activation(st_prob[j % 3], psD[:, j % 4, 0:384], ACT.Exp).then_inc(s["prob"], 1)
                    if i < H:
                        act.wait_ge(s["exp"], i + 1)
                        nc.scalar.activation(st_exp[i % 2], st_exp[i % 2], ACT.Ln, bias=1.0).then_inc(s["ln"], 1)
                    if i >= 5 and (i - 4) % 2 and (i - 5) // 2 * 2 + 1 < H:
                        p = (i - 5) // 2
                        act.wait_ge(s["out"], 2 * p + 2)
                        nc.scalar.activation(oT_hi[:, p, :], psC[:, p % 2, 0:T], ACT.Copy).then_inc(s["ohi"], 1)

            def softmax_attn(w):
                s = sm[w]
                for i in range(H + 5):
                    if i < H:
                        act.wait_ge(s["max"], i + 1)
                        if i >= 3:
                            act.wait_ge(s["turned"], i - 2)
                        for q, (a, b) in enumerate(((0, P), (P, 384))):
                            ins = nc.scalar.activation(sm_p[i % 3][:, a:b], psD[:, i % 2, a:b], ACT.Exp,
                                                       bias=nmx[:, w, i, q:q + 1], accum_out=sums[:, w, i, q:q + 1])
                        if w:
                            ins = nc.scalar.activation(esink[:, i, :], nmx[:, w, i, :], ACT.Exp, bias=sink_bc[:, i:i + 1])
                        ins.then_inc(s["exp"], 1)
                    if 0 <= i - 2 < H:
                        j = i - 2
                        act.wait_ge(s["turned"], j + 1)
                        if j >= 3:
                            act.wait_ge(s["out"], j - 2)
                        nc.scalar.activation(sm_pT[j % 3], psD[:, 2 + j % 2, 0:384], ACT.Copy).then_inc(s["pT"], 1)
                    if i >= 5 and (i - 4) % 2 and (i - 5) // 2 * 2 + 1 < H:
                        p = (i - 5) // 2
                        if w:
                            act.wait_ge(s["gated"], p + 1)
                            src = gated_t[:, p % 2, :]
                        else:
                            act.wait_ge(s["out"], 2 * p + 2)
                            src = psC[:, p % 2, 0:T]
                        nc.scalar.activation(oT_hi[:, p, :], src, ACT.Copy).then_inc(s["ohi"], 1)

            def exp_and_ln():
                act.preload_act_table_set("natural_log_exp_and_others")

            act.wait_ge(rope["arg"], 1)
            nc.scalar.activation(cosin[:, :, :, :], ang[:, 2:4, :, :], ACT.Sin).then_inc(rope["sin"], 1)
            split_to(2)
            act.wait_ge(consts_dve, 1)
            act.wait_ge(small_loaded, 16 * 6)
            exp_and_ln()
            pre(0, [("sb_pre", xT_hi)])
            split_to(3)
            for c in range(4):
                split_to(U0["sb_qk"] + 2 * c + 4)
                if c < 2:
                    evac("sb_qk", c, feature_half(qT, c), scale=QSCALE)
                else:
                    evac("sb_qk", c, feature_half(kT, c - 2))
            for c in range(2):
                split_to(U0["sb_v"] + 2 * c + 4)
                evac("sb_v", c, vt[:, 1, 512 * c:512 * c + 512])
            split_to(U0["sb_o"] + 3)
            stick()
            split_to(U0["ffn0"] + 2)
            post(0)
            pre(1, [("ffn_pre0", xT_hi)])
            conv_ffn(0)
            exp_and_ln()
            split_to(U0["fox_k"] + 2)
            post(1)
            pre(2, [("kv", xT_hi), ("fox_pre", oT_hi)])
            act.wait_ge(forget["bias"], 1)
            settle(nc.scalar.activation(ftmp[:, 1, :], ftmp[:, 1, :], ACT.Exp, scale=-1.0))
            nc.scalar.activation(ftmp[:, 1, :], ftmp[:, 1, :], ACT.Ln, bias=1.0).then_inc(forget["ln"], 1)
            for c in range(2):
                split_to(U0["fox_k"] + 2 * c + 4)
                evac("fox_k", c, feature_half(kT, c))
            for c in range(2):
                split_to(U0["fox_v"] + 2 * c + 4)
                evac("fox_v", c, vt[:, 1, 512 * c:512 * c + 512])
            for c in range(2):
                split_to(U0["fox_q"] + 2 * c + 4)
                evac("fox_q", c, feature_half(qT, c), scale=QSCALE)
            split_to(U0["fox_o"] + 3)
            softmax_attn(0)
            split_to(U0["ffn1"] + 2)
            post(2)
            pre(3, [("ffn_pre1", xT_hi)])
            conv_ffn(1)
            exp_and_ln()
            split_to(U0["at_q"] + 2)
            post(3)
            pre(4, [("at_pre", xT_hi)])
            split_to(U0["at_z"] + 2)
            for c in range(2):
                split_to(U0["at_z"] + 2 * c + 4)
                chunk_wait("at_z", c)
                for a in range(4):
                    k = 4 * c + a
                    ins = nc.scalar.activation(zT[:, k, :], bank(E0["at_z"] + c, a // 2)[:, (a % 2) * T:(a % 2) * T + T],
                                               ACT.Silu, bias=col("bz", k))
                ins.then_inc(chunk_freed_s, 1)
            exp_and_ln()
            split_to(U0["at_o"] + 3)
            softmax_attn(1)
            split_to(U0["rec_f"] + 2)
            post(4)
            pre(5, [("rec_pre", xT_hi)])
            act.wait_ge(rec["v1"], 1)
            settle(nc.scalar.activation(lbv[:, 1, :], lbv[:, 1, :], ACT.Exp, scale=-1.0))
            nc.scalar.activation(lbv[:, 1, :], lbv[:, 1, :], ACT.Ln, bias=1.0).then_inc(rec["s1"], 1)
            for c in range(2):
                split_to(U0["rec_f"] + 2 * c + 4)
                evac("rec_f", c, feature_half(kT, c))

            def log1p_exp(x, n):
                act.wait_ge(rec["v1"], n)
                settle(nc.scalar.activation(x, x, ACT.Exp, scale=-1.0))
                nc.scalar.activation(x, x, ACT.Ln, bias=1.0).then_inc(rec["s1"], 1)

            split_to(U0["rec_q"] + 4)
            evac("rec_q", 0, feature_half(qT, 0))
            log1p_exp(X[0], 2)
            split_to(U0["rec_q"] + 6)
            evac("rec_q", 1, feature_half(qT, 1))
            split_to(U0["rec_z"] + 4)
            evac("rec_z", 0, hn[:, 1, 0:512])
            log1p_exp(X[1], 3)
            split_to(U0["rec_z"] + 6)
            evac("rec_z", 1, hn[:, 1, 512:1024])
            split_to(U0["rec_i"] + 4)
            evac("rec_i", 0, vt[:, 1, 0:512])
            split_to(U0["rec_i"] + 6)
            act.wait_ge(rec["v1"], 4)
            nc.scalar.activation(kk, kk, ACT.Exp).then_inc(rec["s1"], 1)
            act.wait_ge(chunk_freed_v, V_FREED[E0["rec_z"] + 1])
            act.wait_ge(chunk_freed_s, S_FREED[E0["rec_z"] + 1])
            nc.scalar.activation(qT[:, :, :], qT[:, :, :], ACT.Silu).then_inc(rec["silu"], 1)
            nc.scalar.activation(hn[:, :, :], hn[:, :, :], ACT.Silu).then_inc(rec["silu"], 1)
            evac("rec_i", 1, vt[:, 1, 512:1024])
            exp_and_ln()
            act.wait_ge(rec["ready"], 1)
            for li in range(len(LEVELS)):
                act.wait_ge(rec["kdiff"], li + 1)
                act.wait_ge(rec["qdiff"], li + 1)
                nc.scalar.activation(LV, LV, ACT.Exp).then_inc(rec["lexp"], 1)
            act.wait_ge(rec["qdiff"], len(LEVELS) + 1)
            nc.scalar.activation(LV, LV, ACT.Exp).then_inc(rec["lexp"], 1)
            for tt in range(TT):
                act.wait_ge(rec["o"], tt + 1)
                nc.scalar.activation(X[0][:, tt * D:tt * D + D], psD_rows[:, tt, :], ACT.Square).then_inc(rec["osq"], 1)
            act.wait_ge(rec["oss"], 1)
            settle(nc.scalar.activation(rst[:, 1, :], rst[:, 0, :], ACT.Ln, bias=eps_t[:, :], scale=1.0 / P))
            nc.scalar.activation(rst[:, 2, :], rst[:, 1, :], ACT.Exp, scale=-0.5).then_inc(rec["oguess"], 1)
            for b in range(4):
                act.wait_ge(rec["turned"], 2 * b + 2 + KT)
                nc.scalar.activation(oT_hi[:, 2 * b:2 * b + 2, :].rearrange("p k t -> p (k t)"), psC[:, b, :], ACT.Copy).then_inc(rec["ohi"], 1)
            split_to(NU)
            post(5)

        @block.vector
        def _(dve):
            steps = [0]

            def settle(ins):
                ins.then_inc(dve_step, 1)
                steps[0] += 1
                dve.wait_ge(dve_step, steps[0])

            V = nc.vector

            def magnitude(dst, src):
                return V.tensor_scalar(dst.bitcast(I32), src.bitcast(I32), 0x7FFFFFFF, None, ALU.bitwise_and)

            nsplit = [0]

            def split_lo(u, slot, raw_slot):
                dve.wait_ge(hi_done, u + 1)
                V.tensor_tensor(w_lo[:, slot, :], raw[:, raw_slot, :], w_hi[:, slot, :].bitcast(F32),
                                ALU.subtract).then_inc(lo_done, 1)

            def split_to(n):
                for u in range(nsplit[0], min(n, NU)):
                    split_lo(u, u % HL, u % RAW)
                nsplit[0] = max(nsplit[0], min(n, NU))

            def rstd_step(n, tt):
                c = slice(tt, tt + 1)
                dve.wait_ge(norm_ss, TT * n + tt + 1)
                settle(V.tensor_scalar(st[:, n, 3, c], st[:, n, 0, c], 1.0 / D, EPS, ALU.mult, ALU.add))
                dve.wait_ge(norm_guess, TT * n + tt + 1)
                settle(V.scalar_tensor_tensor(st[:, n, 4, c], st[:, n, 2, c], st[:, n, 2, c], st[:, n, 3, c], ALU.mult, ALU.mult))
                settle(V.tensor_scalar(st[:, n, 5, c], st[:, n, 4, c], -0.5, 1.5, ALU.mult, ALU.add))

            def pre(n, gains):
                for tt in range(TT):
                    rstd_step(2 * n, tt)
                    V.tensor_scalar(hn[:, tt, :], h[:, tt, :], st[:, 2 * n, 2, tt:tt + 1], st[:, 2 * n, 5, tt:tt + 1],
                                    ALU.mult, ALU.mult).then_inc(norm_scaled, 1)
                for gi, (gain, hi, lo) in enumerate(gains):
                    for b in range(4):
                        dve.wait_ge(xT_hi_done, xt_base(n) + 4 * gi + (4 if len(gains) > 1 else b + 1))
                        for k in (2 * b, 2 * b + 1):
                            ins = V.scalar_tensor_tensor(lo[:, k, :], psD[:, b, (k % 2) * T:(k % 2) * T + T], col(gain, k),
                                                         hi[:, k, :].bitcast(F32), ALU.mult, ALU.subtract)
                        ins.then_inc(xT_lo_done, 1)

            def post(i):
                n = 2 * i + 1
                if i == 4:
                    for tt in range(TT):
                        dve.wait_ge(unit_done, U0_END[i])
                        V.tensor_tensor(ysb[:, tt, :], psD_rows[:, tt, :], bout_bc, ALU.add).then_inc(ysum, 1)
                dve.wait_ge(gbc_loaded, 16 * (i + 1))
                for tt in range(TT):
                    rstd_step(n, tt)
                    settle(V.tensor_tensor(st[:, n, 4, tt:tt + 1], st[:, n, 5, tt:tt + 1], st[:, n, 2, tt:tt + 1], ALU.mult))
                    src = ysb[:, tt, :] if i == 4 else psD_rows[:, tt, :]
                    settle(V.scalar_tensor_tensor(hn[:, tt, :], src, st[:, n, 4, tt:tt + 1], gbc[:, :], ALU.mult, ALU.mult))
                    V.tensor_tensor(h[:, tt, :], h[:, tt, :], hn[:, tt, :], ALU.add).then_inc(h_new, 1)
                dve.wait_ge(h_new, TT * (i + 1))

            def chunk_wait(name, c):
                dve.wait_ge(unit_done, U0[name] + 2 * c + 2)

            def evac(name, c, dst, scale=None):
                chunk_wait(name, c)
                src = bank(E0[name] + c, 0)
                ins = V.tensor_copy(dst, src) if scale is None else V.tensor_scalar(dst, src, scale, None, ALU.mult)
                ins.then_inc(chunk_freed_v, 1)

            def feature_half(dst, c):
                return dst[:, 4 * c:4 * c + 2, :].rearrange("p k t -> p (k t)")

            def conv_ffn(layer):
                f, u0, e0 = ffn[layer], U0[f"ffn{layer}"], E0[f"ffn{layer}"]

                def taps(j, par, e):
                    for g in range(2):
                        dve.wait_ge(f["centre"], 2 * j + g + 1)
                        for a in range(2):
                            at = PV["conv"] + layer * 176 + (2 * j + a) * 8 + g * 4
                            x = psC[:, 2 * (e % 2) + g, a * T:a * T + T]
                            y = cv[:, par, g, a, :]
                            ins = V.scalar_tensor_tensor(y[:, 1:T], x[:, 0:T - 1], pv[:, bass.ds(at + 1, 1)], y[:, 1:T],
                                                         ALU.mult, ALU.add)
                        ins.then_inc(f["tap1"], 1)
                        dve.wait_ge(f["tap1"], 2 * j + g + 1)
                        for a in range(2):
                            at = PV["conv"] + layer * 176 + (2 * j + a) * 8 + g * 4
                            x = psC[:, 2 * (e % 2) + g, a * T:a * T + T]
                            y = cv[:, par, g, a, :]
                            ins = V.scalar_tensor_tensor(y[:, 2:T], x[:, 0:T - 2], pv[:, bass.ds(at, 1)], y[:, 2:T],
                                                         ALU.mult, ALU.add)
                        ins.then_inc(f["gate"] if g == 0 else chunk_freed_v, 1)

                def product(j, par, freed, peeled):
                    dve.wait_ge(f["gelu"], j + 1)
                    dve.wait_ge(chunk_freed_v, freed)
                    if not peeled or j >= 1:
                        dve.wait_ge(f["g_split"], 2 * j)
                    V.tensor_tensor(gf, ge[:, par, :].rearrange("p (a t) -> p a t", a=2), cv[:, par, 1, :, :],
                                    ALU.mult).then_inc(f["g"], 1)

                for j in range(3):
                    split_to(u0 + 3 * j + 3)
                    taps(j, j % 2, e0 + j)
                    split_to(u0 + 3 * j + 4)
                    product(j, j % 2, V_FREED[e0 + j], True)
                with dve.Fori(0, (NJ - 3) // 2) as i:
                    for par in range(2):
                        j = 2 * i + (3 + par)

                        def split(k):
                            first = u0 + 3 * (3 + par) + k
                            split_lo(first + 6 * i, first % HL, first % RAW)

                        split(1)
                        split(2)
                        taps(j, (3 + par) % 2, e0 + 3 + par)
                        split(3)
                        product(j, (3 + par) % 2, 2 * i + V_FREED[e0 + 3 + par], False)
                nsplit[0] = u0 + 3 * NJ + 1

            def stick():
                s = sz
                for i in range(H + 5):
                    if i < H:
                        dve.wait_ge(s["logit"], i + 1)
                        if i >= 2:
                            dve.wait_ge(s["exp"], i - 1)
                        magnitude(st_abs[i % 2], psD[:, i % 4, 0:384]).then_inc(s["abs"], 1)
                    if 0 <= i - 1 < H:
                        j = i - 1
                        dve.wait_ge(s["ln"], j + 1)
                        if j >= 3:
                            dve.wait_ge(s["later"], j - 2)
                        V.scalar_tensor_tensor(st_keep[j % 3], psD[:, j % 4, 0:384], 0.0, st_exp[j % 2], ALU.max,
                                               ALU.add).then_inc(s["keep"], 1)
                    if i >= 5 and (i - 4) % 2 and (i - 5) // 2 * 2 + 1 < H:
                        p = (i - 5) // 2
                        dve.wait_ge(s["ohi"], p + 1)
                        V.tensor_tensor(oT_lo[:, p, :], psC[:, p % 2, 0:T], oT_hi[:, p, :].bitcast(F32),
                                        ALU.subtract).then_inc(s["olo"], 1)

            def softmax_attn(w):
                s = sm[w]
                for i in range(H + 5):
                    if i < H:
                        dve.wait_ge(s["logit"], i + 1)
                        V.tensor_reduce(mx[:, w, i, 0:1], psD[:, i % 2, 0:P], AX.X, ALU.max)
                        settle(V.tensor_reduce(mx[:, w, i, 1:2], psD[:, i % 2, P:384], AX.X, ALU.max))
                        if w:
                            V.tensor_scalar(nmx[:, w, i, :], mx[:, w, i, :], sink_bc[:, i:i + 1], -1.0, ALU.max,
                                            ALU.mult).then_inc(s["max"], 1)
                        else:
                            V.tensor_scalar(nmx[:, w, i, :], mx[:, w, i, :], -1.0, None, ALU.mult).then_inc(s["max"], 1)
                    if 0 <= i - 1 < H:
                        j = i - 1
                        dve.wait_ge(s["exp"], j + 1)
                        if w:
                            settle(V.tensor_tensor(sums[:, w, j, :], sums[:, w, j, :], esink[:, j, :], ALU.add))
                        settle(V.reciprocal(rsum[:, w, j, :], sums[:, w, j, :]))
                        V.tensor_scalar(sm_p[j % 3][:, 0:P], sm_p[j % 3][:, 0:P], rsum[:, w, j, 0:1], None, ALU.mult)
                        V.tensor_scalar(sm_p[j % 3][:, P:384], sm_p[j % 3][:, P:384], rsum[:, w, j, 1:2], None,
                                        ALU.mult).then_inc(s["norm"], 1)
                    if i >= 5 and (i - 4) % 2 and (i - 5) // 2 * 2 + 1 < H:
                        p = (i - 5) // 2
                        src = psC[:, p % 2, 0:T]
                        if w:
                            dve.wait_ge(s["out"], 2 * p + 2)
                            V.tensor_tensor(gated_t[:, p % 2, :], src, zT[:, p, :], ALU.mult).then_inc(s["gated"], 1)
                            src = gated_t[:, p % 2, :]
                        dve.wait_ge(s["ohi"], p + 1)
                        V.tensor_tensor(oT_lo[:, p, :], src, oT_hi[:, p, :].bitcast(F32), ALU.subtract).then_inc(s["olo"], 1)

            V.memset(ones_row[:, :], 1.0)
            V.memset(eps_t[:, :], EPS).then_inc(consts_dve, 1)
            dve.wait_ge(small_loaded, 16 * 6)
            settle(V.tensor_copy(pos_f[:, :], pos_i[:, :]))
            inv_freq = np.float32(ROPE_THETA) ** (-(np.arange(ROPE_HALF, dtype=np.float32) * np.float32(2.0) / np.float32(2 * ROPE_HALF)))
            for d in range(ROPE_HALF):
                ins = V.tensor_scalar(ang[:, 0, :, d], pos_f[:, :], float(np.float32(inv_freq[d])), None, ALU.mult)
            settle(ins)
            MAGIC = 1.5 * 2.0 ** 23
            settle(V.tensor_scalar(ang[:, 1, :, :], ang[:, 0, :, :], float(1.0 / (2 * np.pi)), MAGIC, ALU.mult, ALU.add))
            settle(V.tensor_scalar(ang[:, 1, :, :], ang[:, 1, :, :], MAGIC, None, ALU.subtract))
            two_pi = 2 * np.pi
            c1 = 6.28125
            c2 = float(np.float32(np.round((two_pi - c1) * 2.0 ** 20) / 2.0 ** 20))
            c3 = float(np.float32(two_pi - c1 - c2))
            for piece in (c1, c2, c3):
                settle(V.scalar_tensor_tensor(ang[:, 0, :, :], ang[:, 1, :, :], -piece, ang[:, 0, :, :], ALU.mult, ALU.add))
            settle(V.tensor_scalar(ang[:, 2, :, :], ang[:, 0, :, :], 3.1415925, -3.1415925, ALU.min, ALU.max))
            settle(magnitude(ang[:, 1, :, :], ang[:, 2, :, :]))
            V.tensor_scalar(ang[:, 3, :, :], ang[:, 1, :, :], -1.0, float(np.float32(np.pi / 2)), ALU.mult,
                            ALU.add).then_inc(rope["arg"], 1)
            split_to(2)
            dve.wait_ge(x_loaded, 16)
            pre(0, [("sb_pre", xT_hi, xT_lo)])
            split_to(3)
            for c in range(4):
                split_to(U0["sb_qk"] + 2 * c + 4)
                if c < 2:
                    evac("sb_qk", c, feature_half(qT, c), QSCALE)
                else:
                    evac("sb_qk", c, feature_half(kT, c - 2))
            for c in range(2):
                split_to(U0["sb_v"] + 2 * c + 4)
                evac("sb_v", c, vt[:, 0, 512 * c:512 * c + 512])
            split_to(U0["sb_o"] + 3)
            stick()
            split_to(U0["ffn0"] + 2)
            post(0)
            pre(1, [("ffn_pre0", xT_hi, xT_lo)])
            conv_ffn(0)
            split_to(U0["fox_k"] + 2)
            post(1)
            pre(2, [("kv", xT_hi, xT_lo), ("fox_pre", oT_hi, oT_lo)])
            dve.wait_ge(forget["product"], 1)
            settle(V.tensor_scalar(ftmp[:, 0, :], psC[0:H, 2 * (E0["fox_k"] % 2) + 1, 0:T], bf_sb[:, :], None, ALU.add))
            magnitude(ftmp[:, 1, :], ftmp[:, 0, :]).then_inc(forget["bias"], 1)
            dve.wait_ge(forget["ln"], 1)
            settle(V.scalar_tensor_tensor(ftmp[:, 2, :], ftmp[:, 0, :], 0.0, ftmp[:, 1, :], ALU.min, ALU.subtract))
            settle(V.tensor_tensor_scan(ftmp[:, 1, :], ones_row[0:H, :], ftmp[:, 2, :], 0.0, ALU.mult, ALU.add))
            V.tensor_scalar(neg_f[:, :], ftmp[:, 1, :], -1.0, None, ALU.mult).then_inc(forget["cum"], 1)
            for c in range(2):
                split_to(U0["fox_k"] + 2 * c + 4)
                evac("fox_k", c, feature_half(kT, c))
            for c in range(2):
                split_to(U0["fox_v"] + 2 * c + 4)
                evac("fox_v", c, vt[:, 0, 512 * c:512 * c + 512])
            for c in range(2):
                split_to(U0["fox_q"] + 2 * c + 4)
                evac("fox_q", c, feature_half(qT, c), QSCALE)
            split_to(U0["fox_o"] + 3)
            softmax_attn(0)
            split_to(U0["ffn1"] + 2)
            post(2)
            pre(3, [("ffn_pre1", xT_hi, xT_lo)])
            conv_ffn(1)
            split_to(U0["at_q"] + 2)
            post(3)
            pre(4, [("at_pre", xT_hi, xT_lo)])
            dve.wait_ge(bias_loaded, 32)
            for c in range(2):
                split_to(U0["at_q"] + 2 * c + 4)
                chunk_wait("at_q", c)
                for tt in range(TT):
                    ins = V.tensor_tensor(qk_tok[:, tt, 512 * c:512 * c + 512], bank(E0["at_q"] + c, tt),
                                          bin_bc[:, 512 * c:512 * c + 512], ALU.add)
                ins.then_inc(chunk_freed_v, 1)
            split_to(U0["at_kv"] + 3)
            dve.wait_ge(unit_done, U0["at_kv"] + 1)
            for tt in range(TT):
                kv = bank(E0["at_kv"], tt)
                V.tensor_tensor(qk_tok[:, tt, D:D + KVW], kv[:, 0:KVW], bin_bc[:, D:D + KVW], ALU.add)
                ins = V.tensor_tensor(vt[:, tt, 0:KVW], kv[:, KVW:2 * KVW], bin_bc[:, D + KVW:D + 2 * KVW], ALU.add)
            ins.then_inc(chunk_freed_v, 1)
            dve.wait_ge(chunk_freed_v, V_FREED[E0["at_kv"]])
            dve.wait_ge(rope["sin"], 1)
            heads = qk_tok.rearrange("p t (h d) -> p t h d", d=DH)
            for tt in range(TT):
                hd = heads[:, tt]
                sin_, cos_ = (cosin[:, i, tt:tt + 1, :].to_broadcast([P, H + 2, ROPE_HALF]) for i in range(2))
                x1, x2 = hd[:, :, 0:ROPE_HALF], hd[:, :, ROPE_HALF:2 * ROPE_HALF]
                t = [rtmp[:, i, 18 * tt:18 * tt + 18, :] for i in range(4)]
                V.tensor_tensor(t[0], x1, cos_, ALU.mult)
                V.tensor_tensor(t[1], x2, sin_, ALU.mult)
                V.tensor_tensor(t[2], x2, cos_, ALU.mult)
                settle(V.tensor_tensor(t[3], x1, sin_, ALU.mult))
                V.tensor_tensor(x1, t[0], t[1], ALU.subtract)
                settle(V.tensor_tensor(x2, t[2], t[3], ALU.add))
            keys = qk_tok[:, :, D:D + KVW].rearrange("p t (g d) -> p t g d", g=2)
            V.tensor_copy(kdup[:, :, :, 0, :], keys)
            V.tensor_copy(kdup[:, :, :, 1, :], keys).then_inc(rope["applied"], 1)
            split_to(U0["at_z"] + 4)
            dve.wait_ge(rope["q_turned"], 1)
            for b in range(4):
                ins = V.tensor_scalar(qT[:, 2 * b:2 * b + 2, :].rearrange("p k t -> p (k t)"), psD[:, b, :], QSCALE, None, ALU.mult)
            ins.then_inc(rope["q_copied"], 1)
            split_to(U0["at_z"] + 6)
            dve.wait_ge(rope["k_turned"], 1)
            V.tensor_copy(kT[:, 0:2, :].rearrange("p k t -> p (k t)"), psC[:, 0, :]).then_inc(rope["k_copied"], 1)
            split_to(U0["at_o"] + 3)
            softmax_attn(1)
            split_to(U0["rec_f"] + 2)
            post(4)
            pre(5, [("rec_pre", xT_hi, xT_lo)])

            settle(V.tensor_tensor(lbv[:, 0, :], col("lb1", 0, 8), col("lb0", 0, 8), ALU.subtract))
            magnitude(lbv[:, 1, :], lbv[:, 0, :]).then_inc(rec["v1"], 1)
            dve.wait_ge(rec["s1"], 1)
            settle(V.scalar_tensor_tensor(lbv[:, 2, :], lbv[:, 0, :], 0.0, lbv[:, 1, :], ALU.min, ALU.subtract))
            settle(V.tensor_tensor(lbv[:, 3, :], lbv[:, 2, :], lbv[:, 0, :], ALU.subtract))
            log_lb, log_rest = lbv[:, 2, :], lbv[:, 3, :]

            def heads3(ap):
                return ap.rearrange("p (k t) -> p k t", t=T)

            for c in range(2):
                split_to(U0["rec_f"] + 2 * c + 4)
                evac("rec_f", c, feature_half(kT, c))
            dve.wait_ge(chunk_freed_s, S_FREED[E0["rec_f"] + 1])
            dve.wait_ge(chunk_freed_v, V_FREED[E0["rec_f"] + 1])
            magnitude(X[0], LV).then_inc(rec["v1"], 1)
            split_to(U0["rec_q"] + 4)
            evac("rec_q", 0, feature_half(qT, 0))
            split_to(U0["rec_q"] + 6)
            dve.wait_ge(rec["s1"], 2)
            settle(V.scalar_tensor_tensor(kk, LV, 0.0, X[0], ALU.min, ALU.subtract))
            settle(V.tensor_tensor(heads3(kk), heads3(kk), bc(log_rest, T), ALU.add))
            evac("rec_q", 1, feature_half(qT, 1))
            split_to(U0["rec_z"] + 4)
            settle(V.tensor_tensor(heads3(cum), heads3(kk), bc(log_lb, T), ALU.subtract))
            magnitude(X[1], cum).then_inc(rec["v1"], 1)
            evac("rec_z", 0, hn[:, 0, 0:512])
            split_to(U0["rec_z"] + 6)
            settle(V.tensor_tensor(heads3(X[0]), heads3(kk), bc(log_lb, T), ALU.max))
            V.tensor_tensor(kk, kk, LV, ALU.subtract).then_inc(rec["v1"], 1)
            evac("rec_z", 1, hn[:, 0, 512:1024])
            split_to(U0["rec_i"] + 4)
            dve.wait_ge(rec["s1"], 3)
            settle(V.tensor_tensor(X[0], X[0], X[1], ALU.add))
            evac("rec_i", 0, vt[:, 0, 0:512])
            split_to(U0["rec_i"] + 6)
            for g in range(TT * REC_H):
                ins = V.tensor_tensor_scan(cum[:, P * g:P * g + P], ones_row[:, 0:P], X[0][:, P * g:P * g + P], 0.0,
                                           ALU.mult, ALU.add)
            settle(ins)
            evac("rec_i", 1, vt[:, 0, 512:1024])
            dve.wait_ge(rec["s1"], 4)
            dve.wait_ge(rec["silu"], 2)
            V.tensor_tensor(hn[:, :, :].rearrange("p t (h v) -> p (t h) v", v=P), hn[:, :, :].rearrange("p t (h v) -> p (t h) v", v=P),
                            gn_bc[:, :].unsqueeze(1).to_broadcast([P, TT * REC_H, P]), ALU.mult).then_inc(dve_step, 1)
            steps[0] += 1
            settle(V.memset(sc_diag, 0.0))
            V.memset(st[:, 0, 4, :], 0.0).then_inc(rec["ready"], 1)
            q_all = qT[:, :, :].rearrange("p k t -> p (k t)")

            def pick(li):
                for half in range(2):
                    dve.wait_ge(rec["level"], 2 * li + half + 1)
                    if li or half:
                        dve.wait_ge(rec["picked"], 2 * li + half)
                    V.copy_predicated(sc_diag[:, 1024 * half:1024 * half + 1024].rearrange("p (g t) -> p g t", t=P),
                                      mask_level[:, li, :].unsqueeze(1).to_broadcast([P, 8, P]),
                                      psD_rows[:, half, :].rearrange("p (g t) -> p g t", t=P)).then_inc(rec["picked"], 1)

            for li, m in enumerate(LEVELS):
                c4, l4, x4, q4 = (level_view(a, m) for a in (cum, LV, X[li % 2], q_all))
                nb = T * REC_H // (2 * m)
                ref = c4[:, :, 0, m - 1:m].to_broadcast([P, nb, m])
                if li >= 1:
                    dve.wait_ge(rec["kx"], li)
                    dve.wait_ge(rec["qx"], li)
                V.tensor_tensor(l4[:, :, 1, :], c4[:, :, 1, :], ref, ALU.subtract).then_inc(rec["qdiff"], 1)
                pick(li)
                dve.wait_ge(rec["lexp"], li + 1)
                if li >= 2:
                    dve.wait_ge(rec["level"], 2 * (li - 2) + 4)
                V.tensor_tensor(x4[:, :, 1, :], l4[:, :, 1, :], q4[:, :, 1, :], ALU.mult).then_inc(rec["qx"], 1)
            NL = len(LEVELS)
            dve.wait_ge(rec["kx"], NL)
            dve.wait_ge(rec["qx"], NL)
            c4, l4 = (level_view(a, P) for a in (cum, LV))
            V.tensor_tensor(l4[:, :, 0, :], c4[:, :, 0, P - 1:P].to_broadcast([P, REC_H, P]), c4[:, :, 0, :], ALU.subtract)
            V.tensor_copy(l4[:, :, 1, :], c4[:, :, 1, :]).then_inc(rec["qdiff"], 1)
            pick(NL)
            dve.wait_ge(rec["lexp"], NL + 1)
            dve.wait_ge(rec["level"], 2 * (NL - 2) + 4)
            x4 = level_view(X[NL % 2], P)
            V.tensor_tensor(x4[:, :, 0, :], l4[:, :, 0, :], level_view(kk, P)[:, :, 0, :], ALU.mult)
            V.tensor_tensor(x4[:, :, 1, :], l4[:, :, 1, :], level_view(q_all, P)[:, :, 1, :], ALU.mult).then_inc(rec["qx"], 1)
            dve.wait_ge(rec["level"], 2 * NL + 3)
            V.tensor_copy(sc_cross, psD_rows[:, 0, :]).then_inc(rec["picked"], 1)
            for tt in range(TT):
                dve.wait_ge(rec["osq"], tt + 1)
                ins = V.tensor_reduce(rst[:, 0, tt * REC_H:tt * REC_H + REC_H],
                                      X[0][:, tt * D:tt * D + D].rearrange("p (h v) -> p h v", v=P), AX.X, ALU.add)
            ins.then_inc(rec["oss"], 1)
            dve.wait_ge(rec["oss"], 1)
            settle(V.tensor_scalar(rst[:, 3, :], rst[:, 0, :], 1.0 / P, EPS, ALU.mult, ALU.add))
            dve.wait_ge(rec["oguess"], 1)
            settle(V.tensor_tensor(rst[:, 4, :], rst[:, 2, :], rst[:, 2, :], ALU.mult))
            settle(V.tensor_tensor(rst[:, 4, :], rst[:, 4, :], rst[:, 3, :], ALU.mult))
            settle(V.tensor_scalar(rst[:, 4, :], rst[:, 4, :], -0.5, 1.5, ALU.mult, ALU.add))
            settle(V.tensor_tensor(rst[:, 5, :], rst[:, 4, :], rst[:, 2, :], ALU.mult))
            for tt in range(TT):
                og = X[1][:, tt * D:tt * D + D].rearrange("p (h v) -> p h v", v=P)
                settle(V.tensor_tensor(og, psD_rows[:, tt, :].rearrange("p (h v) -> p h v", v=P),
                                       bc(rst[:, 5, tt * REC_H:tt * REC_H + REC_H], P), ALU.mult))
                V.tensor_tensor(X[1][:, tt * D:tt * D + D], X[1][:, tt * D:tt * D + D], hn[:, tt, :], ALU.mult).then_inc(rec["gated"], 1)
            for b in range(4):
                dve.wait_ge(rec["ohi"], b + 1)
                dst = oT_lo[:, 2 * b:2 * b + 2, :].rearrange("p k t -> p (k t)")
                V.tensor_tensor(dst, psC[:, b, :], oT_hi[:, 2 * b:2 * b + 2, :].rearrange("p k t -> p (k t)").bitcast(F32),
                                ALU.subtract).then_inc(rec["olo"], 1)
            split_to(NU)
            post(5)

        @block.tensor
        def _(pe):
            MM = nc.tensor.matmul

            def product3(out, lhs, rhs, start, stop):
                MM(out, lhs[0], rhs[0], start=start, stop=False, skip_group_check=True)
                MM(out, lhs[0], rhs[1], start=False, stop=False, skip_group_check=True)
                return MM(out, lhs[1], rhs[0], start=False, stop=stop, skip_group_check=True)

            def turn(n):
                if n == 0:
                    pe.wait_ge(consts_pool, N_CONSTS)
                for tt in range(TT):
                    pe.wait_ge(norm_scaled, TT * n + tt + 1)
                    for k in range(KT):
                        if n and not tt:
                            pe.wait_ge(h_new, TT * n)
                        at = (k % 2) * T + tt * P
                        nc.tensor.transpose(psD[:, k // 2, at:at + P], hn[:, tt, k * P:k * P + P], ident[:, :]).then_inc(xT_turned, 1)

            def wait_banks(e):
                if e >= 2:
                    pe.wait_ge(chunk_freed_v, V_FREED[e - 2])
                    pe.wait_ge(chunk_freed_s, S_FREED[e - 2])

            def features_half(u, uslot, e, half, xt):
                hi = w_hi[:, uslot, :].rearrange("p (k n) -> p k n", k=4)
                lo = w_lo[:, uslot, :].rearrange("p (k n) -> p k n", k=4)
                pe.wait_ge(lo_done, u + 1)
                for a in range(4):
                    out = psC[:, 2 * (e % 2) + a // 2, (a % 2) * T:(a % 2) * T + T]
                    for k in range(4):
                        kk_ = 4 * half + k
                        ins = product3(out, (hi[:, k, a * P:a * P + P], lo[:, k, a * P:a * P + P]),
                                       (xt[0][:, kk_, :], xt[1][:, kk_, :]), start=(kk_ == 0 and a % 2 == 0),
                                       stop=(kk_ == KT - 1))
                ins.then_inc(unit_done, 1)

            def features(name, n, xt, first=0):
                for c in range(first, n):
                    e = E0[name] + c
                    wait_banks(e)
                    for half in range(2):
                        u = U0[name] + 2 * c + half
                        features_half(u, u % HL, e, half, xt)

            def tokens_half(u, outs, half, xt):
                hi = unit_hi(u).rearrange("p (k n) -> p k n", k=4)
                lo = unit_lo(u).rearrange("p (k n) -> p k n", k=4)
                pe.wait_ge(lo_done, u + 1)
                for tt in range(TT):
                    for k in range(4):
                        kk_ = 4 * half + k
                        ins = product3(outs[tt], (xt[0][:, kk_, tt * P:tt * P + P], xt[1][:, kk_, tt * P:tt * P + P]),
                                       (hi[:, k, :], lo[:, k, :]), start=(kk_ == 0), stop=(kk_ == KT - 1))
                ins.then_inc(unit_done, 1)

            def tokens(name, n, xt):
                for c in range(n):
                    e = E0[name] + c
                    wait_banks(e)
                    for half in range(2):
                        tokens_half(U0[name] + 2 * c + half, [bank(e, tt) for tt in range(TT)], half, xt)

            def gather(name, xt):
                for c in range(2):
                    for half in range(2):
                        tokens_half(U0[name] + 2 * c + half, [psD[:, 2 * tt + c, :] for tt in range(TT)], half, xt)

            def conv_ffn(layer):
                f, u0, e0 = ffn[layer], U0[f"ffn{layer}"], E0[f"ffn{layer}"]
                xt = (xT_hi, xT_lo)

                def down(d, u, uslot, par, first, last):
                    hi = w_hi[:, uslot, :].rearrange("p (k n) -> p k n", k=2)
                    lo = w_lo[:, uslot, :].rearrange("p (k n) -> p k n", k=2)
                    pe.wait_ge(lo_done, u + 1)
                    pe.wait_ge(f["g_split"], 2 * d + 2)
                    for tt in range(TT):
                        for c in range(2):
                            for k in range(2):
                                ins = product3(psD[:, 2 * tt + c, :],
                                               (gT_hi[:, par, k, tt * P:tt * P + P], gT_lo[:, par, k, tt * P:tt * P + P]),
                                               (hi[:, k, 512 * c:512 * c + 512], lo[:, k, 512 * c:512 * c + 512]),
                                               start=(first and k == 0), stop=(last and k == 1))
                    ins.then_inc(unit_done, 1)

                for j in range(3):
                    e, u = e0 + j, u0 + 3 * j - (1 if j else 0)
                    wait_banks(e)
                    for half in range(2):
                        features_half(u + half, (u + half) % HL, e, half, xt)
                    if j:
                        down(j - 1, u + 2, (u + 2) % HL, (j - 1) % 2, j == 1, False)
                with pe.Fori(0, (NJ - 3) // 2) as i:
                    for par in range(2):
                        j0 = 3 + par
                        first = u0 + 3 * j0 - 1
                        pe.wait_ge(chunk_freed_v, 2 * i + V_FREED[e0 + j0 - 2])
                        for half in range(2):
                            features_half(first + half + 6 * i, (first + half) % HL, e0 + j0, half, xt)
                        down(2 * i + (j0 - 1), first + 2 + 6 * i, (first + 2) % HL, (j0 - 1) % 2, False, False)
                u = u0 + 3 * NJ - 1
                down(NJ - 1, u, u % HL, (NJ - 1) % 2, False, True)

            def stick():
                s = sz
                pe.wait_ge(chunk_freed_v, V_FREED[E0["sb_v"] + 1])
                pe.wait_ge(chunk_freed_s, S_FREED[E0["sb_v"] + 1])
                for i in range(H + 3):
                    if i < H:
                        p0, k = DH * (i % 2), i // 2
                        if i >= 4:
                            pe.wait_ge(s["prob"], i - 3)
                        z = psD[:, i % 4, :]
                        MM(z[:, 0:384], ident_b[:, :], mask_stick[:, :], start=True, stop=False, skip_group_check=True)
                        MM(z[:, 0:T], kT[p0:p0 + DH, k, 0:P], qT[p0:p0 + DH, k, :], start=False, stop=False, skip_group_check=True)
                        MM(z[:, T:384], kT[p0:p0 + DH, k, P:T], qT[p0:p0 + DH, k, P:T], start=False, stop=False,
                           skip_group_check=True).then_inc(s["logit"], 1)
                    if 0 <= i - 2 < H:
                        j = i - 2
                        pe.wait_ge(s["keep"], j + 1)
                        z, kp = psD[:, j % 4, :], st_keep[j % 3]
                        MM(z[:, 0:384], neg_tri[:, :], kp, start=False, stop=False, skip_group_check=True)
                        MM(z[:, P:T], neg_ones[:, :], kp[:, T:384], start=False, stop=True,
                           skip_group_check=True).then_inc(s["later"], 1)
                    if 0 <= i - 3 < H:
                        j = i - 3
                        pe.wait_ge(s["prob"], j + 1)
                        if j % 2 == 0 and j >= 4:
                            pe.wait_ge(s["olo"], j // 2 - 1)
                        value(j, st_prob[j % 3], j * DH).then_inc(s["out"], 1)

            def value(j, probT, vcol):
                p0 = DH * (j % 2)
                o = psC[p0:p0 + DH, (j // 2) % 2, 0:T]
                MM(o, vt[:, 0, vcol:vcol + DH], probT[:, 0:T], start=True, stop=False, skip_group_check=True)
                return MM(o[:, P:T], vt[:, 1, vcol:vcol + DH], probT[:, T:384], start=False, stop=True, skip_group_check=True)

            def softmax_attn(w):
                s = sm[w]
                for i in range(H + 4):
                    if i < H:
                        p0, k = DH * (i % 2), i // 2
                        kk_ = i // 8 if w else k
                        if i >= 2:
                            pe.wait_ge(s["exp"], i - 1)
                        z = psD[:, i % 2, :]
                        MM(z[:, 0:384], ident_b[:, :], (mask_window if w else mask_causal)[:, :], start=True, stop=False,
                           skip_group_check=True)
                        if not w:
                            MM(z[:, 0:P], sel[:, i, :], neg_f[:, 0:P], start=False, stop=False, skip_group_check=True)
                            MM(z[:, P:384], sel[:, i, :], neg_f[:, :], start=False, stop=False, skip_group_check=True)
                        MM(z[:, 0:P], qT[p0:p0 + DH, k, 0:P], kT[p0:p0 + DH, kk_, 0:P], start=False, stop=False, skip_group_check=True)
                        MM(z[:, P:384], qT[p0:p0 + DH, k, P:T], kT[p0:p0 + DH, kk_, :], start=False, stop=True,
                           skip_group_check=True).then_inc(s["logit"], 1)
                    if 0 <= i - 2 < H:
                        j = i - 2
                        pe.wait_ge(s["norm"], j + 1)
                        if j >= 2:
                            pe.wait_ge(s["pT"], j - 1)
                        for b in range(3):
                            ins = nc.tensor.transpose(psD[:, 2 + j % 2, P * b:P * b + P], sm_p[j % 3][:, P * b:P * b + P], ident[:, :])
                        ins.then_inc(s["turned"], 1)
                    if 0 <= i - 3 < H:
                        j = i - 3
                        pe.wait_ge(s["pT"], j + 1)
                        if j % 2 == 0 and j >= 4:
                            pe.wait_ge(s["olo"], j // 2 - 1)
                        value(j, sm_pT[j % 3], (j // 8 if w else j) * DH).then_inc(s["out"], 1)

            xt = (xT_hi, xT_lo)
            ot = (oT_hi, oT_lo)
            turn(0)
            pe.wait_ge(xT_lo_done, xt_base(1))
            features("sb_qk", 4, xt)
            tokens("sb_v", 2, xt)
            stick()
            pe.wait_ge(sz["olo"], H // 2)
            gather("sb_o", ot)
            turn(1)
            pe.wait_ge(xT_lo_done, xt_base(2))
            conv_ffn(0)
            turn(2)
            pe.wait_ge(xT_lo_done, xt_base(2) + 4)
            wait_banks(E0["fox_k"])
            for k in range(KT):
                out_f = psC[0:H, 2 * (E0["fox_k"] % 2) + 1, 0:T]
                MM(out_f, wf_sb[:, k, :], xT_hi[:, k, :].bitcast(F32), start=(k == 0), stop=False, skip_group_check=True)
                ins = MM(out_f, wf_sb[:, k, :], xT_lo[:, k, :].bitcast(F32), start=False, stop=(k == KT - 1), skip_group_check=True)
            ins.then_inc(forget["product"], 1)
            pe.wait_ge(forget["bias"], 1)
            features("fox_k", 2, xt)
            tokens("fox_v", 2, xt)
            pe.wait_ge(xT_lo_done, xt_base(3))
            features("fox_q", 2, ot)
            pe.wait_ge(chunk_freed_v, V_FREED[E0["fox_q"] + 1])
            pe.wait_ge(chunk_freed_s, S_FREED[E0["fox_q"] + 1])
            pe.wait_ge(forget["cum"], 1)
            softmax_attn(0)
            pe.wait_ge(sm[0]["olo"], H // 2)
            gather("fox_o", ot)
            turn(3)
            pe.wait_ge(xT_lo_done, xt_base(4))
            conv_ffn(1)
            turn(4)
            pe.wait_ge(xT_lo_done, xt_base(5))
            tokens("at_q", 2, xt)
            e, u = E0["at_kv"], U0["at_kv"]
            wait_banks(e)
            pe.wait_ge(lo_done, u + 1)
            hi8, lo8 = (a.rearrange("p (k n) -> p k n", k=KT) for a in (unit_hi(u), unit_lo(u)))
            for tt in range(TT):
                for k in range(KT):
                    ins = product3(bank(e, tt)[:, 0:256], (xT_hi[:, k, tt * P:tt * P + P], xT_lo[:, k, tt * P:tt * P + P]),
                                   (hi8[:, k, :], lo8[:, k, :]), start=(k == 0), stop=(k == KT - 1))
            ins.then_inc(unit_done, 1)
            features("at_z", 2, xt)
            pe.wait_ge(rope["applied"], 1)
            for k in range(KT):
                for tt in range(TT):
                    at = (k % 2) * T + tt * P
                    ins = nc.tensor.transpose(psD[:, k // 2, at:at + P], qk_tok[:, tt, k * P:k * P + P], ident[:, :])
            ins.then_inc(rope["q_turned"], 1)
            pe.wait_ge(chunk_freed_s, S_FREED[E0["at_z"] + 1])
            for g in range(2):
                for tt in range(TT):
                    at = g * T + tt * P
                    ins = nc.tensor.transpose(psC[:, 0, at:at + P], kdup[:, tt, g, :, :].rearrange("p r d -> p (r d)"), ident[:, :])
            ins.then_inc(rope["k_turned"], 1)
            pe.wait_ge(rope["q_copied"], 1)
            pe.wait_ge(rope["k_copied"], 1)
            softmax_attn(1)
            pe.wait_ge(sm[1]["olo"], H // 2)
            gather("at_o", ot)
            turn(5)
            pe.wait_ge(xT_lo_done, xt_base(6))
            features("rec_f", 2, xt)
            features("rec_q", 2, xt)
            tokens("rec_z", 2, xt)
            tokens("rec_i", 2, xt)
            pe.wait_ge(rec["ready"], 1)
            NL = len(LEVELS)
            for li in range(NL + 1):
                for half in range(2):
                    if li:
                        pe.wait_ge(rec["kx"], li)
                        pe.wait_ge(rec["qx"], li)
                        pe.wait_ge(rec["picked"], 2 * (li - 1) + half + 1)
                    for g in range(8):
                        tile = 8 * half + g
                        if li:
                            a = b = X[(li - 1) % 2][:, P * tile:P * tile + P]
                        else:
                            a = kk[:, P * tile:P * tile + P]
                            b = qT[:, tile // 2, P * (tile % 2):P * (tile % 2) + P]
                        ins = MM(psD[:, 2 * half + g // 4, P * (g % 4):P * (g % 4) + P], a, b, start=(g % 4 == 0), stop=True,
                                 skip_group_check=True)
                    ins.then_inc(rec["level"], 1)
            pe.wait_ge(rec["qx"], NL + 1)
            pe.wait_ge(rec["picked"], 2 * NL + 1)
            for g in range(REC_H):
                xg = X[NL % 2]
                ins = MM(psD[:, g // 4, P * (g % 4):P * (g % 4) + P], xg[:, T * g:T * g + P], xg[:, T * g + P:T * g + T],
                         start=(g % 4 == 0), stop=True, skip_group_check=True)
            ins.then_inc(rec["level"], 1)
            pe.wait_ge(rec["picked"], 2 * NL + 3)
            pe.wait_ge(chunk_freed_v, V_FREED[E0["rec_i"] + 1])
            pe.wait_ge(chunk_freed_s, S_FREED[E0["rec_i"] + 1])
            for tt in range(TT):
                for g in range(REC_H):
                    o = psD[:, 2 * tt + g // 4, P * (g % 4):P * (g % 4) + P]
                    s_tile = 2 * g + tt
                    ins = MM(o, sc_diag[:, P * s_tile:P * s_tile + P], vt[:, tt, P * g:P * g + P], start=(g % 4 == 0),
                             stop=(tt == 0), skip_group_check=True)
                    if tt:
                        ins = MM(o, sc_cross[:, P * g:P * g + P], vt[:, 0, P * g:P * g + P], start=False, stop=True,
                                 skip_group_check=True)
                ins.then_inc(rec["o"], 1)
            for tt in range(TT):
                pe.wait_ge(rec["gated"], tt + 1)
                for k in range(KT):
                    at = (k % 2) * T + tt * P
                    nc.tensor.transpose(psC[:, k // 2, at:at + P], X[1][:, tt * D + k * P:tt * D + k * P + P],
                                        ident[:, :]).then_inc(rec["turned"], 1)
            pe.wait_ge(rec["olo"], 4)
            gather("rec_o", ot)


N_CONSTS = 3 + 1 + 6 + 1 + 1 + 7
U0_END = [U0["sb_o"] + 4, U0["ffn0"] + 3 * NJ, U0["fox_o"] + 4, U0["ffn1"] + 3 * NJ, U0["at_o"] + 4, U0["rec_o"] + 4]


def xt_base(n):
    return 4 * n + (4 if n > 2 else 0)


def column_units(w):
    n = w.shape[1] // 512
    return np.ascontiguousarray(w.reshape(2, 4, P, n, 512).transpose(3, 0, 2, 1, 4)).reshape(2 * n, P, UNIT)


def ffn_units(up, down):
    cols = np.stack([up[:, :FF].reshape(D, NJ, 256), up[:, FF:].reshape(D, NJ, 256)], axis=2)
    ups = column_units(cols.reshape(D, NJ * 512)).reshape(NJ, 2, P, UNIT)
    downs = down.reshape(NJ, 2, P, D).transpose(0, 2, 1, 3).reshape(NJ, P, UNIT)
    order = [ups[0, 0], ups[0, 1]]
    for j in range(1, NJ):
        order += [ups[j, 0], ups[j, 1], downs[j - 1]]
    order.append(downs[NJ - 1])
    return np.stack(order)


def per_partition(v):
    return v.reshape(-1, P).T


def kernel(**a):
    import concourse.bacc as bacc
    from concourse.bass_utils import run_bass_kernel_spmd

    a = {k: np.asarray(v) for k, v in a.items()}
    w_kvf, w_at, w_rec = a["w_kvf"], a["attn_w_in_2"][0], a["rec_w_in_2"][0]
    kv_cols = w_at[:, D:D + 256].reshape(KT, P, 256).transpose(1, 0, 2).reshape(1, P, UNIT)
    stream = np.concatenate([
        column_units(a["sb_w_qkv"][0]), column_units(a["sb_w_o"][0]), ffn_units(a["w_up"][0], a["w_down"][0]),
        column_units(w_kvf[:, :2 * D]), column_units(a["fox_w_q"][0]), column_units(a["fox_w_o"][0]),
        ffn_units(a["w_up"][1], a["w_down"][1]),
        column_units(w_at[:, :D]), kv_cols, column_units(w_at[:, D + 256:]), column_units(a["attn_w_out_2"][0]),
        column_units(w_rec[:, D:2 * D]), column_units(w_rec[:, :D]), column_units(w_rec[:, 3 * D:]),
        column_units(w_rec[:, 2 * D:3 * D]), column_units(a["rec_w_out_2"][0])])
    conv = np.concatenate([a["conv_w"], a["conv_b"][:, None, :]], axis=1)
    conv = conv.reshape(2, 4, 2, FF // P, P).transpose(4, 0, 3, 2, 1).reshape(P, -1)
    pvec = np.concatenate([
        per_partition(a["sb_pre_g"][0]), per_partition(a["kv_norm_g"]), per_partition(a["fox_pre_g"][0]),
        per_partition(a["ffn_pre_g"][0]), per_partition(a["ffn_pre_g"][1]), per_partition(a["pre_norm_w_2"][0]),
        per_partition(a["pre_norm_w_2"][1]), per_partition(a["attn_b_in_2"][0][D + 256:]),
        per_partition(a["rec_lb_logits_2"][0]), per_partition(a["rec_lb_logits_2"][1]), conv], axis=1)
    post_g = np.stack([a["sb_post_g"][0], a["ffn_post_g"][0], a["fox_post_g"][0], a["ffn_post_g"][1],
                       a["post_norm_w_2"][0], a["post_norm_w_2"][1]])
    arrays = {
        "stream": stream, "pvec": pvec, "post_g": post_g, "x_in": a["x"],
        "wf": w_kvf[:, 2 * D:].reshape(KT, P, H).transpose(1, 0, 2), "bf": a["b_f"].reshape(H, 1),
        "b_in": a["attn_b_in_2"][0][:D + 256], "b_out": a["attn_b_out_2"][0], "sinks": a["attn_sinks_2"][0],
        "gnorm": a["rec_gnorm_w_2"][0], "pos": a["positions_2"].reshape(TT, P).T}
    arrays = {k: np.ascontiguousarray(v) for k, v in arrays.items()}

    nc = bacc.Bacc("TRN2", target_bir_lowering=False, num_devices=1)
    args = [nc.dram_tensor(k, v.shape, mybir.dt.from_np(v.dtype), kind="ExternalInput").ap() for k, v in arrays.items()]
    out = nc.dram_tensor("out", (1, T, D), F32, kind="ExternalOutput").ap()
    build(nc, *args, out)
    r = run_bass_kernel_spmd(nc, [arrays], core_ids=[0])
    return r.results[0]["out"]
```

```python
from contextlib import ExitStack

import numpy as np
import concourse.bass as bass
from concourse import mybir

F32 = mybir.dt.float32
F32R = mybir.dt.float32r
BF16 = mybir.dt.bfloat16
I32 = mybir.dt.int32
I8 = mybir.dt.int8
ALU = mybir.AluOpType
ACT = mybir.ActivationFunctionType
AX = mybir.AxisListType

P = 128
D = 1024
T = 256
TT = T // P
KT = D // P
H = 16
F2 = 48
DH = D // H
FF = 2816
NJ = FF // 256
KVW = 128
REC_H = 8
EPS = 1e-6
QSCALE = DH ** -0.5
NEG = -1e30
ROPE_HALF = 8
ROPE_THETA = 500000.0
UNIT = 2048
RAW = 3
HL = 3

PLAN = [("sb_qk", "T", 4), ("sb_v", "tok", 2), ("sb_o", "o", 2), ("ffn0", "ffn", NJ),
        ("fox_k", "T", 2), ("fox_v", "tok", 2), ("fox_q", "T", 2), ("fox_o", "o", 2), ("ffn1", "ffn", NJ),
        ("at_q", "tok", 2), ("at_kv", "narrow", 1), ("at_z", "T", 2), ("at_o", "o", 2),
        ("rec_f", "T", 2), ("rec_q", "T", 2), ("rec_z", "tok", 2), ("rec_i", "tok", 2), ("rec_o", "o", 2)]
UNITS_OF = {"T": 2, "tok": 2, "narrow": 1, "o": 2, "ffn": 3}
BY = {"tok": "VS", "narrow": "V", "T": "V", "ffn": ""}
BY_STAGE = {"at_q": "V"}

U0, E0 = {}, {}
V_FREED, S_FREED = [], []
_u = _v = _s = 0
for _name, _kind, _n in PLAN:
    U0[_name], E0[_name] = _u, len(V_FREED)
    _u += UNITS_OF[_kind] * _n
    if _kind != "o":
        for _c in range(_n):
            _by = BY_STAGE.get(_name, BY[_kind])
            _v += "V" in _by
            _s += "S" in _by
            V_FREED.append(_v)
            S_FREED.append(_s)
NU = _u

PV = {}
_c = 0
for _name, _n in [("sb_pre", 8), ("kv", 8), ("fox_pre", 8), ("ffn_pre0", 8), ("ffn_pre1", 8), ("at_pre", 8),
                  ("rec_pre", 8), ("bz", 8), ("lb0", 8), ("lb1", 8), ("conv", 2 * 22 * 2 * 4)]:
    PV[_name] = _c
    _c += _n
NPV = _c


def build(nc, stream, pvec, post_g, x_in, wf, bf, b_in, b_out, sinks, gnorm, pos, out):
    with ExitStack() as ctx:
        def sb(name, shape, dt=F32):
            return ctx.enter_context(nc.sbuf_tensor(name, shape, dt))

        def sem(name):
            return ctx.enter_context(nc.semaphore(name))

        raw = sb("raw", [P, RAW, UNIT])
        w_hi = sb("w_hi", [P, HL, UNIT], F32R)
        w_lo = sb("w_lo", [P, HL, UNIT], F32R)
        xT_hi = sb("xT_hi", [P, KT, T], F32R)
        xT_lo = sb("xT_lo", [P, KT, T], F32R)
        oT_hi = sb("oT_hi", [P, KT, T], F32R)
        oT_lo = sb("oT_lo", [P, KT, T], F32R)
        h = sb("h", [P, TT, D])
        hn = sb("hn", [P, TT, D])
        qT = sb("qT", [P, KT, T])
        kT = sb("kT", [P, KT, T])
        vt = sb("vt", [P, TT, D])
        gbc = sb("gbc", [P, D])
        pv = sb("pv", [P, NPV])
        arena = sb("arena", [P, 11264])
        ident = sb("ident", [P, P])
        ident_b = sb("ident_b", [P, P], BF16)
        neg_tri = sb("neg_tri", [P, P])
        neg_ones = sb("neg_ones", [P, P])
        neg_tri_r = sb("neg_tri_r", [P, P], F32R)
        neg_ones_r = sb("neg_ones_r", [P, P], F32R)
        mask_stick = sb("mask_stick", [P, 384], BF16)
        mask_causal = sb("mask_causal", [P, 384], BF16)
        mask_window = sb("mask_window", [P, 384], BF16)
        mask_level = sb("mask_level", [P, 8, P], I8)
        bf_sb = sb("bf_sb", [F2, 1])
        ones_row = sb("ones_row", [P, T])
        scale_diag = sb("scale_diag", [P, T])
        scale_row = sb("scale_row", [P, T])
        sink_bc = sb("sink_bc", [P, H])
        gn_bc = sb("gn_bc", [P, P])
        pos_i = sb("pos_i", [P, TT], I32)
        pos_f = sb("pos_f", [P, TT])
        ang = sb("ang", [P, 4, TT, ROPE_HALF])
        cosin = sb("cosin", [P, 2, TT, ROPE_HALF])
        eps_t = sb("eps_t", [P, 1])
        st = sb("st", [P, 12, 9, TT])
        nmx = sb("nmx", [P, 2, H, 2])
        mx = sb("mx", [P, 2, H, 2])
        sums = sb("sums", [P, 2, H, 2])
        esink = sb("esink", [P, H, 2])
        rsum = sb("rsum", [P, 2, H, 2])
        lbv = sb("lbv", [P, 5, KT])
        rst = sb("rst", [P, 6, TT * REC_H])

        psC = ctx.enter_context(nc.psum_tensor("psC", [P, 4, 512], F32))
        psD = ctx.enter_context(nc.psum_tensor("psD", [P, 4, 512], F32))
        psD_rows = psD[:, :, :].rearrange("p (t b) n -> p t (b n)", t=TT)

        raw_loaded = [sem(f"raw_loaded{i}") for i in range(RAW)]
        hi_done = sem("hi_done")
        lo_done = sem("lo_done")
        unit_done = sem("unit_done")
        chunk_freed_v = sem("chunk_freed_v")
        chunk_freed_s = sem("chunk_freed_s")
        x_loaded = [sem(f"x_loaded{i}") for i in range(TT)]
        pv_loaded = sem("pv_loaded")
        small_loaded = sem("small_loaded")
        gbc_loaded = sem("gbc_loaded")
        bias_loaded = sem("bias_loaded")
        ident_made = sem("ident_made")
        consts_pool = sem("consts_pool")
        ones_made = sem("ones_made")
        consts_act = sem("consts_act")
        consts_dve = sem("consts_dve")
        act_step = sem("act_step")
        dve_step = sem("dve_step")
        pool_step = sem("pool_step")
        norm_ss = sem("norm_ss")
        norm_half = sem("norm_half")
        norm_guess = sem("norm_guess")
        row_scale = sem("row_scale")
        diag_made = sem("diag_made")
        scale_spread = sem("scale_spread")
        raw_kept = sem("raw_kept")
        rows_done = sem("rows_done")
        xT_turned = sem("xT_turned")
        xT_hi_done = sem("xT_hi_done")
        xT_lo_done = sem("xT_lo_done")
        h_new = sem("h_new")
        ysum = sem("ysum")
        sz = {n: sem(f"stick_{n}") for n in ("logit", "abs_odd", "abs_even", "exp", "ln", "keep", "split", "later", "prob", "out", "ohi", "olo")}
        sm = [{n: sem(f"{s}_{n}") for n in ("logit", "max", "exp", "norm", "turned", "pT", "out", "gated", "ohi", "olo")}
              for s in ("fox", "win")]
        forget = {n: sem(f"forget_{n}") for n in ("product", "bias", "exp", "ln", "cum")}
        rope = {n: sem(f"rope_{n}") for n in ("arg", "sin", "z", "silu", "applied", "q_turned", "q_copied", "k_turned", "k_copied")}
        ffn = [{n: sem(f"ffn{i}_{n}") for n in ("scaled", "centre", "tap1", "gate", "up", "gelu", "g", "g_hi", "g_lo")} for i in range(2)]
        rec = {n: sem(f"rec_{n}") for n in ("v1", "s1", "silu", "cleared", "kk", "ready", "kdiff", "qdiff", "kexp", "qexp",
                                            "kx", "qx", "level", "cross", "crossed", "picked", "o", "osq", "oguess", "gated", "turned", "ohi", "olo")}
        stored = sem("stored")

        block = ctx.enter_context(nc.Block())

        def region(at, n):
            return arena[:, at:at + n]

        st_abs = [region(384 * i, 384) for i in range(2)]
        st_exp = [region(768 + 384 * i, 384) for i in range(2)]
        st_keep = [region(1536 + 384 * i, 384) for i in range(3)]
        st_prob = [region(2688 + 384 * i, 384) for i in range(3)]
        sm_p = [region(384 * i, 384) for i in range(5)]
        sm_pT = [region(1920 + 384 * i, 384) for i in range(3)]
        flat = [a[:, :, :].rearrange("p k t -> p (k t)") for a in (xT_hi, xT_lo)]
        st_khi, st_klo = ([a[:, 384 * i:384 * i + 384] for i in range(3)] for a in flat)
        wf_sb = region(4608, KT * F2).rearrange("p (k n) -> p k n", k=KT)
        wf_hi, wf_lo = (a[:, 4:6, :].rearrange("p k t -> p (k t)")[:, 0:KT * F2].rearrange("p (k n) -> p k n", k=KT)
                        for a in (oT_hi, oT_lo))
        sel = arena[:, 5632:7680].rearrange("p (h n) -> p h n", h=H)
        ftmp = arena[0:F2, 8576:9344].rearrange("p (i t) -> p i t", t=T)
        neg_f = flat[1][:, 0:T]
        sel_r = flat[0].rearrange("p (h n) -> p h n", h=H)
        cv = region(0, 2048).rearrange("p (b g a t) -> p b g a t", b=2, g=2, a=2)
        ge = region(2048, 1024).rearrange("p (b n) -> p b n", b=2)
        gf = region(3072, 512)
        xs = region(3584, 1024).rearrange("p (g a t) -> p g a t", g=2, a=2)
        qk_tok = region(2304, 2304).rearrange("p (t w) -> p t w", t=TT)
        kdup = region(4608, 512).rearrange("p (t g r d) -> p t g r d", t=TT, g=2, r=2)
        rtmp = region(5120, 1152).rearrange("p (i n d) -> p i n d", i=4, d=ROPE_HALF)
        bin_bc = region(6272, 1280)
        bout_bc = region(7552, 1024)
        ysb = region(8576, 2048).rearrange("p (t n) -> p t n", t=TT)
        gated_t = region(10624, 512).rearrange("p (b n) -> p b n", b=2)
        cum = region(0, 2048)
        kk = region(2048, 2048)
        X = [region(4096, 2048), region(6144, 2048)]
        sc_diag = region(8192, 2048)
        sc_cross = region(10240, 1024)
        LV = kT[:, :, :].rearrange("p k t -> p (k t)")
        hn_T = hn[:, :, :].rearrange("p t (k n) -> p (t k) n", n=T)
        zT = hn[:, :, :].rearrange("p t (k n) -> p (t k) n", n=T)
        gT_hi = oT_hi[:, 0:4, :].rearrange("p (b a) t -> p b a t", b=2)
        gT_lo = oT_lo[:, 0:4, :].rearrange("p (b a) t -> p b a t", b=2)

        def col(name, i=0, n=1):
            return pv[:, PV[name] + i:PV[name] + i + n]

        def bank(e, b):
            return psC[:, 2 * (e % 2) + b, :]

        def unit_hi(u):
            return w_hi[:, u % HL, :]

        def unit_lo(u):
            return w_lo[:, u % HL, :]

        def post_steps(i):
            steps_ = [(tt, c) for tt in range(TT) for c in range(2)]
            return steps_ if i in (1, 3) else sorted(steps_, key=lambda step: step[::-1])

        def squares(n, tt, c):
            steps_ = post_steps(n // 2) if n % 2 else post_steps(1)
            return 2 * TT * n + steps_.index((tt, c)) + 1

        def stick_bank(i):
            return psD[:, i % 6, :] if i % 6 < 4 else psC[:, i % 6 - 2, :]

        def rows_wait(i, tt, c):
            if i in (1, 3):
                done = 2 * tt + c + 1
                return (rows_done, ROWS0[i] + done) if done < 4 else (unit_done, U0_END[i])
            if c == 0:
                return unit_done, U0_END[i] - 2
            return (rows_done, ROWS0[i] + 1) if tt == 0 else (unit_done, U0_END[i])

        def xbank(n, b):
            return (2 * (E_FIRST[n] % 2) + b) % 4

        def level_view(ap, m):
            return ap.rearrange("p (b two m) -> p b two m", two=2, m=m)

        def bc(ap2, n):
            return ap2.unsqueeze(2).to_broadcast([ap2.shape[0], ap2.shape[1], n])

        PRE = {"sb": 0, "ffn0": 1, "fox": 2, "ffn1": 3, "at": 4, "rec": 5}
        LEVELS = [64, 32, 16, 8, 4, 2, 1, P]

        @block.sync
        def _(sp):
            for tt in range(TT):
                sp.dma_start(h[:, tt, :], x_in[0, tt * P:tt * P + P, :]).then_inc(x_loaded[tt], 16)
            for u in range(RAW):
                sp.dma_start(raw[:, u, :], stream[u]).then_inc(raw_loaded[u], 16)

            def load(u, slot):
                sp.wait_ge(lo_done, u - RAW + 1)
                sp.dma_start(raw[:, slot, :], stream[u]).then_inc(raw_loaded[slot], 16)

            whole = NU // RAW
            with sp.Fori(1, whole) as i:
                for s in range(RAW):
                    load(i * RAW + s, s)
            for u in range(whole * RAW, NU):
                load(u, u % RAW)
            for tt in range(TT):
                for c in range(2):
                    sp.wait_ge(h_new, 2 * TT * 5 + 2 * tt + c + 1)
                    sp.dma_start(out[0, tt * P:tt * P + P, 512 * c:512 * c + 512], h[:, tt, 512 * c:512 * c + 512]).then_inc(stored, 16)
            sp.wait_ge(stored, 16 * 2 * TT)

        @block.gpsimd
        def _(pool):
            nc.gpsimd.memset(ident[:, :], 0.0).then_inc(pool_step, 1)
            pool.wait_ge(pool_step, 1)
            nc.gpsimd.affine_select(out=ident[:, :], in_=ident[:, :], compare_op=ALU.not_equal, fill=1.0, base=0,
                                    pattern=[[-1, P]], channel_multiplier=1).then_inc(ident_made, 1)
            nc.gpsimd.memset(wf_sb, 0.0).then_inc(pool_step, 1)
            nc.gpsimd.memset(bf_sb[:, :], 0.0).then_inc(pool_step, 1)
            pool.wait_ge(pool_step, 3)
            nc.gpsimd.memset(neg_ones[:, :], -1.0).then_inc(ones_made, 1)
            for dst, src in ((pos_i[:, :], pos), (wf_sb[:, :, 0:H], wf), (wf_sb[:, :, 32:F2], wf), (bf_sb[0:H, :], bf), (bf_sb[32:F2, :], bf),
                             (sink_bc[:, :], sinks.partition_broadcast(P)), (gn_bc[:, :], gnorm.partition_broadcast(P))):
                pool.dma_start(dst, src).then_inc(small_loaded, 16)
            pool.dma_start(gbc[:, :], post_g[0].partition_broadcast(P)).then_inc(gbc_loaded, 16)

            fills = [(ident_b, 0.0), (neg_tri, -1.0), (mask_stick, 0.0),
                     (mask_causal, 0.0), (mask_window, 0.0)]
            for t, value in fills:
                nc.gpsimd.memset(t[:, :], value).then_inc(pool_step, 1)
            nc.gpsimd.memset(sel, 0.0).then_inc(pool_step, 1)
            nc.gpsimd.memset(mask_level[:, :, :], 0).then_inc(pool_step, 1)
            done = len(fills) + 5
            pool.wait_ge(pool_step, done)
            for li, m in enumerate(LEVELS[:7]):
                half = level_view(mask_level[:, li + 1, :], m)[:, :, 1, :]
                nc.gpsimd.memset(half, 1).then_inc(pool_step, 1)
                done += 1
            pool.wait_ge(pool_step, done)

            def keep(view, op, fill, base, pattern, mult):
                return nc.gpsimd.affine_select(out=view, in_=view, compare_op=op, fill=fill, base=base,
                                               pattern=pattern, channel_multiplier=mult)

            keep(ident_b[:, :], ALU.not_equal, 1.0, 0, [[-1, P]], 1).then_inc(consts_pool, 1)
            keep(mask_level[:, 0, :], ALU.not_equal, 1.0, 0, [[-1, P]], 1).then_inc(consts_pool, 1)
            keep(neg_tri[:, :], ALU.is_ge, 0.0, 0, [[-1, P]], 1).then_inc(consts_pool, 1)
            for a in (0, 256):
                keep(mask_stick[:, a:a + P], ALU.is_gt, NEG, 0, [[1, P]], -1).then_inc(consts_pool, 1)
                keep(mask_causal[:, a:a + P], ALU.is_ge, NEG, 0, [[-1, P]], 1).then_inc(consts_pool, 1)
                keep(mask_window[:, a:a + P], ALU.is_ge, NEG, 0, [[-1, P]], 1).then_inc(consts_pool, 1)
            keep(mask_window[:, P:2 * P], ALU.is_gt, NEG, 0, [[1, P]], -1).then_inc(consts_pool, 1)
            for base in (0, -32):
                keep(sel, ALU.not_equal, 1.0, base, [[-1, H], [0, P]], 1).then_inc(pool_step, 1)
                done += 1
                pool.wait_ge(pool_step, done)
            for li, m in enumerate(LEVELS[:7]):
                half = level_view(mask_level[:, li + 1, :], m)[:, :, 1, :]
                keep(half, ALU.is_ge, 0.0, 0, [[-2 * m, P // (2 * m)], [0, m]], 1).then_inc(pool_step, 1)
                done += 1
            pool.wait_ge(pool_step, done)
            for li, m in enumerate(LEVELS[:7]):
                half = level_view(mask_level[:, li + 1, :], m)[:, :, 1, :]
                keep(half, ALU.is_ge, 0.0, m - 1, [[2 * m, P // (2 * m)], [0, m]], -1).then_inc(consts_pool, 1)

            def next_gain(i):
                pool.wait_ge(h_new, 2 * TT * i)
                pool.dma_start(gbc[:, :], post_g[i].partition_broadcast(P)).then_inc(gbc_loaded, 16)

            for i in range(1, 5):
                next_gain(i)
            pool.dma_start(bin_bc, b_in.partition_broadcast(P)).then_inc(bias_loaded, 16)
            pool.dma_start(bout_bc, b_out.partition_broadcast(P)).then_inc(bias_loaded, 16)
            next_gain(5)

            nc.gpsimd.memset(sc_diag, 0.0).then_inc(rec["cleared"], 1)
            pool.wait_ge(rec["v1"], 4)
            nc.gpsimd.tensor_tensor(kk, kk, LV, ALU.subtract).then_inc(rec["kk"], 1)
            pool.wait_ge(rec["ready"], 1)
            for li, m in enumerate(LEVELS):
                c4, l4, x4, k4 = (level_view(a, m) for a in (cum, LV, X[li % 2], kk))
                nb = T * REC_H // (2 * m)
                ref = c4[:, :, 0, m - 1:m].to_broadcast([P, nb, m])
                if li >= 1:
                    pool.wait_ge(rec["kx"], li)
                    pool.wait_ge(rec["qx"], li)
                nc.gpsimd.tensor_tensor(l4[:, :, 0, :], ref, c4[:, :, 0, :], ALU.subtract).then_inc(rec["kdiff"], 1)
                pool.wait_ge(rec["kexp"], li + 1)
                if li >= 2:
                    pool.wait_ge(rec["level"], 2 * li)
                nc.gpsimd.tensor_tensor(x4[:, :, 0, :], l4[:, :, 0, :], k4[:, :, 0, :], ALU.mult).then_inc(rec["kx"], 1)

        @block.scalar
        def _(act):
            steps = [0]

            def settle(ins):
                ins.then_inc(act_step, 1)
                steps[0] += 1
                act.wait_ge(act_step, steps[0])

            nsplit = [0]

            def split_hi(u, slot, raw_slot, loads, peeled):
                act.wait_ge(raw_loaded[raw_slot], 16 * loads)
                if not peeled or u >= HL:
                    act.wait_ge(unit_done, u - HL + 1)
                nc.scalar.activation(w_hi[:, slot, :], raw[:, raw_slot, :], ACT.Copy).then_inc(hi_done, 1)

            def split_to(n):
                for u in range(nsplit[0], min(n, NU)):
                    split_hi(u, u % HL, u % RAW, u // RAW + 1, True)
                nsplit[0] = max(nsplit[0], min(n, NU))

            def split_quarter(u, q):
                cols = slice(512 * q, 512 * q + 512)
                if q == 0:
                    assert u == nsplit[0]
                    act.wait_ge(raw_loaded[u % RAW], 16 * (u // RAW + 1))
                    act.wait_ge(unit_done, u - HL + 1)
                ins = nc.scalar.activation(w_hi[:, u % HL, cols], raw[:, u % RAW, cols], ACT.Copy)
                if q == 3:
                    ins.then_inc(hi_done, 1)
                    nsplit[0] = u + 1

            def mean_square(n, tt, c, src, junk):
                nc.scalar.activation(junk, src, ACT.Square, scale=D ** -0.5,
                                     accum_out=st[:, n, c, tt:tt + 1]).then_inc(norm_ss, 1)
                if c:
                    act.wait_ge(norm_ss, squares(n, tt, c))
                    act.wait_ge(norm_half, TT * n + tt + 1)
                    settle(nc.scalar.activation(st[:, n, 5, tt:tt + 1], st[:, n, 1, tt:tt + 1], ACT.Ln, bias=st[:, n, 2, tt:tt + 1]))
                    nc.scalar.activation(st[:, n, 6, tt:tt + 1], st[:, n, 5, tt:tt + 1], ACT.Exp, scale=-0.5).then_inc(norm_guess, 1)

            def junk(tt, c):
                return kT[:, 4 * tt:4 * tt + 4, :].rearrange("p k t -> p (k t)")[:, 512 * c:512 * c + 512]

            def pre(n, gain):
                for b in range(4):
                    act.wait_ge(xT_turned, KT * TT * n + KT + 2 * b + 2)
                    src = psC[:, xbank(n, b), :]
                    for k in (2 * b, 2 * b + 1):
                        ins = nc.scalar.activation(xT_hi[:, k, :], src[:, (k % 2) * T:(k % 2) * T + T], ACT.Copy,
                                                   scale=col(gain, k))
                    ins.then_inc(xT_hi_done, 1)
                    if n == 2 and b == 3:
                        for kept in range(4):
                            act.wait_ge(xT_lo_done, xt_base(n) + kept + 1)
                            nc.scalar.activation(hn_T[:, 2 * kept:2 * kept + 2, :].rearrange("p k t -> p (k t)"),
                                                 psC[:, xbank(n, kept), :], ACT.Copy).then_inc(raw_kept, 1)

            def pre_stats(n):
                for tt in range(TT):
                    for c in range(2):
                        mean_square(2 * n, tt, c, h[:, tt, 512 * c:512 * c + 512], junk(tt, c))

            def post(i):
                for q, (tt, c) in enumerate(post_steps(i)):
                    if i == 4:
                        act.wait_ge(ysum, q + 1)
                        src = ysb[:, tt, 512 * c:512 * c + 512]
                    else:
                        act.wait_ge(*rows_wait(i, tt, c))
                        src = psD[:, 2 * tt + c, :]
                    mean_square(2 * i + 1, tt, c, src, junk(tt, c))

            def chunk_wait(name, c):
                act.wait_ge(unit_done, U0[name] + 2 * c + 2)

            def evac(name, c, dst, n):
                chunk_wait(name, c)
                act.wait_ge(row_scale, TT * n + 2)
                nc.scalar.activation(dst, bank(E0[name] + c, 1), ACT.Copy, scale=st[:, 2 * n, 4, 1:2]).then_inc(chunk_freed_s, 1)

            def conv_ffn(layer):
                f, u0, e0 = ffn[layer], U0[f"ffn{layer}"], E0[f"ffn{layer}"]
                act.preload_act_table_set("gelu_apprx_tanh_and_others")

                def centre(j, par):
                    for g in range(2):
                        act.wait_ge(f["scaled"], 2 * j + g + 1)
                        for a in range(2):
                            at = PV["conv"] + layer * 176 + (2 * j + a) * 8 + g * 4
                            ins = nc.scalar.activation(cv[:, par, g, a, :], xs[:, g, a, :], ACT.Identity,
                                                       scale=pv[:, bass.ds(at + 2, 1)], bias=pv[:, bass.ds(at + 3, 1)])
                        ins.then_inc(f["centre"], 1)

                def gelu(j, par):
                    act.wait_ge(f["gate"], j + 1)
                    nc.scalar.activation(ge[:, par, :], cv[:, par, 0, :, :].rearrange("p a t -> p (a t)"),
                                         ACT.Gelu_apprx_tanh).then_inc(f["gelu"], 1)

                def gate_hi(j, par, peeled):
                    act.wait_ge(f["g"], j + 1)
                    if not peeled or j >= 2:
                        act.wait_ge(unit_done, u0 + 3 * j - 1 + (2 if peeled and j == NJ - 1 else 0))
                    nc.scalar.activation(gT_hi[:, par].rearrange("p a t -> p (a t)"), gf, ACT.Copy).then_inc(f["g_hi"], 1)

                def chunk(j):
                    if j < NJ - 1:
                        split_to(u0 + 3 * j + (3 if j else 4))
                    centre(j, j % 2)
                    if j == NJ - 1:
                        split_to(u0 + 3 * NJ)
                    if j < NJ - 1:
                        split_to(u0 + 3 * j + 4)
                    gelu(j, j % 2)
                    if j < NJ - 1:
                        split_to(u0 + 3 * j + 5)
                    gate_hi(j, j % 2, True)

                for j in range(3):
                    chunk(j)
                    if layer == 0 and j == 0:
                        act.wait_ge(small_loaded, 16 * 7)
                        nc.scalar.activation(wf_hi, wf_sb, ACT.Copy).then_inc(consts_act, 1)
                with act.Fori(0, (NJ - 5) // 2) as i:
                    for par in range(2):
                        j = 2 * i + (3 + par)

                        def split(k):
                            first = u0 + 3 * (3 + par) + k
                            split_hi(first + 6 * i, first % HL, first % RAW, i * (6 // RAW) + (first // RAW + 1), False)

                        split(2)
                        centre(j, (3 + par) % 2)
                        split(3)
                        gelu(j, (3 + par) % 2)
                        split(4)
                        gate_hi(j, (3 + par) % 2, False)
                nsplit[0] = u0 + 3 * (NJ - 2) + 2
                for j in (NJ - 2, NJ - 1):
                    chunk(j)

            def stick():
                s = sz
                for i in range(H + 6):
                    if 2 <= i < 6:
                        split_quarter(U0["sb_o"] + 2, i - 2)
                    if i < H:
                        if i % 2:
                            act.wait_ge(s["abs_odd"], i // 2 + 1)
                        else:
                            act.wait_ge(s["logit"], i + 1)
                            if i >= 2:
                                act.wait_ge(s["exp"], i - 1)
                            nc.scalar.activation(st_abs[i % 2], stick_bank(i)[:, 0:384], ACT.Abs).then_inc(s["abs_even"], 1)
                            act.wait_ge(s["abs_even"], i // 2 + 1)
                        if i >= 2:
                            act.wait_ge(s["keep"], i - 1)
                        nc.scalar.activation(st_exp[i % 2], st_abs[i % 2], ACT.Exp, scale=-1.0).then_inc(s["exp"], 1)
                    if 0 <= i - 3 < H:
                        j = i - 3
                        act.wait_ge(s["later"], j + 1)
                        if j >= 3:
                            act.wait_ge(s["out"], j - 2)
                        nc.scalar.activation(st_prob[j % 3], stick_bank(j)[:, 0:384], ACT.Exp).then_inc(s["prob"], 1)
                    if i < H:
                        act.wait_ge(s["exp"], i + 1)
                        nc.scalar.activation(st_exp[i % 2], st_exp[i % 2], ACT.Ln, bias=1.0).then_inc(s["ln"], 1)
                    if i >= 6 and i % 2 == 0 and (i - 6) // 2 * 2 + 1 < H:
                        p = (i - 6) // 2
                        act.wait_ge(s["out"], 2 * p + 2)
                        nc.scalar.activation(oT_hi[:, p, :], psC[:, p % 2, 0:T], ACT.Copy).then_inc(s["ohi"], 1)

            def softmax_attn(w):
                s = sm[w]
                for i in range(H + 6):
                    if 2 <= i < 6:
                        split_quarter(U0[("fox_o", "at_o")[w]] + 2, i - 2)
                    if i < H:
                        act.wait_ge(s["max"], i + 1)
                        if i >= 5:
                            act.wait_ge(s["turned"], i - 4)
                        for q, (a, b) in enumerate(((0, P), (P, 384))):
                            ins = nc.scalar.activation(sm_p[i % 5][:, a:b], psD[:, i % 4, a:b], ACT.Exp,
                                                       bias=nmx[:, w, i, q:q + 1], accum_out=sums[:, w, i, q:q + 1])
                        if w:
                            ins = nc.scalar.activation(esink[:, i, :], nmx[:, w, i, :], ACT.Exp, bias=sink_bc[:, i:i + 1])
                        ins.then_inc(s["exp"], 1)
                    if 0 <= i - 3 < H:
                        j = i - 3
                        act.wait_ge(s["turned"], j + 1)
                        if j >= 3:
                            act.wait_ge(s["out"], j - 2)
                        nc.scalar.activation(sm_pT[j % 3], psC[:, 2 + j % 2, 0:384], ACT.Copy).then_inc(s["pT"], 1)
                    if i >= 6 and i % 2 == 0 and (i - 6) // 2 * 2 + 1 < H:
                        p = (i - 6) // 2
                        if w:
                            act.wait_ge(s["gated"], p + 1)
                            src = gated_t[:, p % 2, :]
                        else:
                            act.wait_ge(s["out"], 2 * p + 2)
                            src = psC[:, p % 2, 0:T]
                        nc.scalar.activation(oT_hi[:, p, :], src, ACT.Copy).then_inc(s["ohi"], 1)

            def exp_and_ln():
                act.preload_act_table_set("natural_log_exp_and_others")

            act.dma_start(pv[:, :], pvec).then_inc(pv_loaded, 16)
            exp_and_ln()
            act.wait_ge(pv_loaded, 16)
            act.wait_ge(consts_dve, 1)
            pre(0, "sb_pre")
            split_to(U0["sb_qk"] + 2)
            pre_stats(0)
            split_to(4)
            act.wait_ge(consts_pool, N_CONSTS)
            nc.scalar.activation(neg_tri_r[:, :], neg_tri[:, :], ACT.Copy).then_inc(consts_act, 1)
            act.wait_ge(ones_made, 1)
            nc.scalar.activation(neg_ones_r[:, :], neg_ones[:, :], ACT.Copy).then_inc(consts_act, 1)
            act.wait_ge(rope["arg"], 1)
            nc.scalar.activation(cosin[:, :, :, :], ang[:, 2:4, :, :], ACT.Sin).then_inc(rope["sin"], 1)
            exp_and_ln()
            split_to(U0["sb_v"] + 2)
            for c in range(2):
                split_to(U0["sb_v"] + 2 * c + 4)
                evac("sb_v", c, vt[:, 1, 512 * c:512 * c + 512], 0)
            stick()
            split_to(U0["ffn0"] + 1)
            post(0)
            pre(1, "ffn_pre0")
            split_to(U0["ffn0"] + 2)
            pre_stats(1)
            conv_ffn(0)
            split_to(U0["fox_k"] + 1)
            exp_and_ln()
            post(1)
            pre(2, "kv")
            split_to(U0["fox_k"] + 2)
            pre_stats(2)
            split_to(U0["fox_k"] + 4)
            act.wait_ge(forget["product"], 1)
            for k in range(KT):
                act.wait_ge(raw_kept, k // 2 + 1)
                nc.scalar.activation(oT_hi[:, k, :], hn_T[:, k, :], ACT.Copy, scale=col("fox_pre", k)).then_inc(xT_hi_done, 1)
            split_to(U0["fox_v"] + 2)
            act.wait_ge(forget["bias"], 1)
            settle(nc.scalar.activation(ftmp[:, 1, :], ftmp[:, 1, :], ACT.Exp, scale=-1.0))
            nc.scalar.activation(ftmp[:, 1, :], ftmp[:, 1, :], ACT.Ln, bias=1.0).then_inc(forget["ln"], 1)
            for c in range(2):
                split_to(U0["fox_v"] + 2 * c + 4)
                evac("fox_v", c, vt[:, 1, 512 * c:512 * c + 512], 2)
            split_to(U0["fox_o"] + 2)
            softmax_attn(0)
            split_to(U0["ffn1"] + 1)
            post(2)
            pre(3, "ffn_pre1")
            split_to(U0["ffn1"] + 2)
            pre_stats(3)
            conv_ffn(1)
            split_to(U0["at_q"] + 1)
            exp_and_ln()
            post(3)
            pre(4, "at_pre")
            split_to(U0["at_q"] + 2)
            pre_stats(4)
            split_to(U0["at_o"] + 2)
            for k in range(KT):
                act.wait_ge(rope["z"], k // 2 + 1)
                nc.scalar.activation(zT[:, k, :], zT[:, k, :], ACT.Silu, bias=col("bz", k)).then_inc(rope["silu"], 1)
            exp_and_ln()
            softmax_attn(1)
            split_to(U0["rec_f"] + 1)
            post(4)
            pre(5, "rec_pre")
            split_to(U0["rec_f"] + 2)
            pre_stats(5)
            split_to(U0["rec_f"] + 3)
            act.wait_ge(rec["v1"], 1)
            settle(nc.scalar.activation(lbv[:, 1, :], lbv[:, 1, :], ACT.Exp, scale=-1.0))
            nc.scalar.activation(lbv[:, 1, :], lbv[:, 1, :], ACT.Ln, bias=1.0).then_inc(rec["s1"], 1)

            def log1p_exp(x, n):
                act.wait_ge(rec["v1"], n)
                settle(nc.scalar.activation(x, x, ACT.Exp, scale=-1.0))
                nc.scalar.activation(x, x, ACT.Ln, bias=1.0).then_inc(rec["s1"], 1)

            split_to(U0["rec_q"] + 3)
            log1p_exp(X[0], 2)
            split_to(U0["rec_q"] + 5)
            log1p_exp(X[1], 3)
            split_to(U0["rec_q"] + 7)
            act.wait_ge(rec["kk"], 1)
            for k in range(KT):
                ins = nc.scalar.activation(kk[:, T * k:T * k + T], kk[:, T * k:T * k + T], ACT.Exp, bias=lbv[:, 3, k:k + 1])
            ins.then_inc(rec["s1"], 1)
            act.wait_ge(chunk_freed_v, V_FREED[E0["rec_q"] + 1])
            nc.scalar.activation(qT[:, :, :], qT[:, :, :], ACT.Silu).then_inc(rec["silu"], 1)
            exp_and_ln()

            def level_exps(li):
                m = LEVELS[li]
                l4, q4 = level_view(LV, m), level_view(cum if m == P else LV, m)
                act.wait_ge(rec["qdiff"], li + 1)
                nc.scalar.activation(l4[:, :, 1, :], q4[:, :, 1, :], ACT.Exp).then_inc(rec["qexp"], 1)
                act.wait_ge(rec["kdiff"], li + 1)
                nc.scalar.activation(l4[:, :, 0, :], l4[:, :, 0, :], ACT.Exp).then_inc(rec["kexp"], 1)

            for i, (name, c, dst) in enumerate((("rec_z", 0, hn[:, 1, 0:512]), ("rec_z", 1, hn[:, 1, 512:1024]),
                                                ("rec_i", 0, vt[:, 1, 0:512]), ("rec_i", 1, vt[:, 1, 512:1024]))):
                u = U0[name] + 2 * c
                split_to(u + 3)
                if i == 3:
                    act.wait_ge(chunk_freed_v, V_FREED[E0["rec_z"] + 1])
                    act.wait_ge(chunk_freed_s, S_FREED[E0["rec_z"] + 1])
                    nc.scalar.activation(hn[:, :, :], hn[:, :, :], ACT.Silu).then_inc(rec["silu"], 1)
                    exp_and_ln()
                if i:
                    level_exps(2 * i - 1)
                split_to(u + 4)
                level_exps(2 * i)
                evac(name, c, dst, 5)
            level_exps(7)
            for tt in range(TT):
                act.wait_ge(rec["o"], tt + 1)
                if tt == 0:
                    act.wait_ge(rec["level"], 16)
                for g in range(REC_H):
                    at = tt * D + g * P
                    ins = nc.scalar.activation(X[0][:, at:at + P], psD[:, 2 * tt + g // 4, P * (g % 4):P * (g % 4) + P], ACT.Square,
                                               accum_out=rst[:, 0, tt * REC_H + g:tt * REC_H + g + 1])
                    if g % 4 == 3:
                        ins.then_inc(rec["osq"], 1)
                r = slice(tt * REC_H, tt * REC_H + REC_H)
                act.wait_ge(rec["osq"], 2 * tt + 2)
                settle(nc.scalar.activation(rst[:, 1, r], rst[:, 0, r], ACT.Ln, bias=eps_t[:, :], scale=1.0 / P))
                nc.scalar.activation(rst[:, 2, r], rst[:, 1, r], ACT.Exp, scale=-0.5).then_inc(rec["oguess"], 1)
            for b in range(4):
                act.wait_ge(rec["turned"], 2 * b + 2 + KT)
                nc.scalar.activation(oT_hi[:, 2 * b:2 * b + 2, :].rearrange("p k t -> p (k t)"), psC[:, b, :], ACT.Copy).then_inc(rec["ohi"], 1)
            split_to(NU)
            post(5)

        @block.vector
        def _(dve):
            steps = [0]

            def settle(ins):
                ins.then_inc(dve_step, 1)
                steps[0] += 1
                dve.wait_ge(dve_step, steps[0])

            V = nc.vector

            def magnitude(dst, src):
                return V.tensor_scalar(dst.bitcast(I32), src.bitcast(I32), 0x7FFFFFFF, None, ALU.bitwise_and)

            nsplit = [0]

            def split_lo(u, slot, raw_slot):
                dve.wait_ge(hi_done, u + 1)
                V.tensor_tensor(w_lo[:, slot, :], raw[:, raw_slot, :], w_hi[:, slot, :].bitcast(F32),
                                ALU.subtract).then_inc(lo_done, 1)

            def split_to(n):
                for u in range(nsplit[0], min(n, NU)):
                    split_lo(u, u % HL, u % RAW)
                nsplit[0] = max(nsplit[0], min(n, NU))

            def split_quarter(u, q):
                cols = slice(512 * q, 512 * q + 512)
                if q == 0:
                    assert u == nsplit[0]
                    dve.wait_ge(hi_done, u + 1)
                ins = V.tensor_tensor(w_lo[:, u % HL, cols], raw[:, u % RAW, cols], w_hi[:, u % HL, cols].bitcast(F32), ALU.subtract)
                if q == 3:
                    ins.then_inc(lo_done, 1)
                    nsplit[0] = u + 1

            def half_mean(n, tt):
                at = slice(tt, tt + 1)
                dve.wait_ge(norm_ss, squares(n, tt, 0))
                V.tensor_scalar(st[:, n, 2, at], st[:, n, 0, at], EPS, None, ALU.add).then_inc(norm_half, 1)

            def row_scales(n, tt):
                at = slice(tt, tt + 1)
                dve.wait_ge(norm_ss, squares(n, tt, 1))
                dve.wait_ge(norm_half, TT * n + tt + 1)
                V.tensor_tensor(st[:, n, 3, at], st[:, n, 1, at], st[:, n, 2, at], ALU.add)
                dve.wait_ge(norm_guess, TT * n + tt + 1)
                y = st[:, n, 6, at]
                settle(V.tensor_scalar(st[:, n, 7, at], y, -0.5, None, ALU.mult))
                settle(V.scalar_tensor_tensor(st[:, n, 8, at], y, y, st[:, n, 3, at], ALU.mult, ALU.mult))
                return V.scalar_tensor_tensor(st[:, n, 4, at], st[:, n, 8, at], 3.0, st[:, n, 7, at], ALU.subtract, ALU.mult)

            def pre(n, gain):
                for b in range(4):
                    dve.wait_ge(xT_hi_done, xt_base(n) + b + 1)
                    for k in (2 * b, 2 * b + 1):
                        ins = V.scalar_tensor_tensor(xT_lo[:, k, :], psC[:, xbank(n, b), (k % 2) * T:(k % 2) * T + T], col(gain, k),
                                                     xT_hi[:, k, :].bitcast(F32), ALU.mult, ALU.subtract)
                    ins.then_inc(xT_lo_done, 1)

            def pre_scales(n):
                for tt in range(TT):
                    half_mean(2 * n, tt)
                    row_scales(2 * n, tt).then_inc(row_scale, 1)
                dve.wait_ge(row_scale, TT * n + 2)
                if n == 0:
                    dve.wait_ge(ident_made, 1)
                for tt in range(TT):
                    V.tensor_scalar(scale_diag[:, tt * P:tt * P + P], ident[:, :], st[:, 2 * n, 4, tt:tt + 1], None,
                                    ALU.mult).then_inc(diag_made, 1)

            def pre_spread(n):
                dve.wait_ge(scale_spread, n + 1)
                settle(V.tensor_scalar(scale_row[:, :], psD[:, 0, 0:T], -1.0, None, ALU.mult))

            def post(i):
                n = 2 * i + 1
                dve.wait_ge(gbc_loaded, 16 * (i + 1))
                for q, (tt, c) in enumerate(post_steps(i)):
                    cols = slice(512 * c, 512 * c + 512)
                    if i == 4:
                        dve.wait_ge(*rows_wait(i, tt, c))
                        V.tensor_tensor(ysb[:, tt, cols], psD[:, 2 * tt + c, :], bout_bc[:, cols], ALU.add).then_inc(ysum, 1)
                        dve.wait_ge(ysum, q + 1)
                        src = ysb[:, tt, cols]
                    else:
                        dve.wait_ge(norm_ss, squares(n, tt, c))
                        src = psD[:, 2 * tt + c, :]
                    V.tensor_tensor(hn[:, tt, cols], src, gbc[:, cols], ALU.mult)
                    if c == 0:
                        half_mean(n, tt)
                        continue
                    settle(row_scales(n, tt))
                    for half in range(2):
                        cols = slice(512 * half, 512 * half + 512)
                        V.scalar_tensor_tensor(h[:, tt, cols], hn[:, tt, cols], st[:, n, 4, tt:tt + 1], h[:, tt, cols], ALU.mult,
                                               ALU.add).then_inc(h_new, 1)

            def chunk_wait(name, c):
                dve.wait_ge(unit_done, U0[name] + 2 * c + 2)

            def evac(name, c, dst, n):
                chunk_wait(name, c)
                V.tensor_scalar(dst, bank(E0[name] + c, 0), st[:, 2 * n, 4, 0:1], None, ALU.mult).then_inc(chunk_freed_v, 1)

            def along(ap, a=2):
                return ap.rearrange("p (a t) -> p a t", a=a)

            row_bc = scale_row[:, :].unsqueeze(1).to_broadcast([P, 2, T])

            def evac_features(name, c, dst, scale=None, signal=None, first=0):
                chunk_wait(name, c)
                for b in range(2):
                    k = 4 * (c - first) + 2 * b
                    src, out_ = along(bank(E0[name] + c, b)), dst[:, k:k + 2, :]
                    if scale is None:
                        ins = V.tensor_tensor(out_, src, row_bc, ALU.mult)
                    else:
                        ins = V.scalar_tensor_tensor(out_, src, scale, row_bc, ALU.mult, ALU.mult)
                    if signal is not None and b == 0:
                        ins.then_inc(signal, 1)
                ins.then_inc(chunk_freed_v, 1)
                if signal is not None:
                    dve.wait_ge(chunk_freed_v, V_FREED[E0[name] + c])
                    V.memset(st[:, 0, 3, :], 0.0).then_inc(signal, 1)

            def conv_ffn(layer):
                f, u0, e0 = ffn[layer], U0[f"ffn{layer}"], E0[f"ffn{layer}"]

                def scaled(j, e, up_done):
                    dve.wait_ge(unit_done, up_done)
                    for g in range(2):
                        V.tensor_tensor(xs[:, g], along(psC[:, 2 * (e % 2) + g, :]), row_bc, ALU.mult).then_inc(f["scaled"], 1)

                def taps(j, par):
                    for g in range(2):
                        dve.wait_ge(f["centre"], 2 * j + g + 1)
                        for back, name in ((1, "tap1"), (2, "gate" if g == 0 else "up")):
                            for a in range(2):
                                at = PV["conv"] + layer * 176 + (2 * j + a) * 8 + g * 4
                                y = cv[:, par, g, a, back:T]
                                ins = V.scalar_tensor_tensor(y, xs[:, g, a, 0:T - back], pv[:, bass.ds(at + 2 - back, 1)], y,
                                                             ALU.mult, ALU.add)
                            ins.then_inc(f[name], 1)
                            if back == 1:
                                dve.wait_ge(f["tap1"], 2 * j + g + 1)

                def product(j, par):
                    dve.wait_ge(f["gelu"], j + 1)
                    dve.wait_ge(f["up"], j + 1)
                    V.tensor_tensor(gf, ge[:, par, :], cv[:, par, 1, :, :].rearrange("p a t -> p (a t)"),
                                    ALU.mult).then_inc(f["g"], 1)

                def gate_lo(j, par):
                    dve.wait_ge(f["g_hi"], j + 1)
                    V.tensor_tensor(gT_lo[:, par].rearrange("p a t -> p (a t)"), gf,
                                    gT_hi[:, par].rearrange("p a t -> p (a t)").bitcast(F32), ALU.subtract).then_inc(f["g_lo"], 1)

                def chunk(j):
                    if j < NJ - 1:
                        split_to(u0 + 3 * j + (3 if j else 4))
                    scaled(j, e0 + j, u0 + 3 * j + (2 if j == 0 else 0 if j == NJ - 1 else 1))
                    taps(j, j % 2)
                    if j < NJ - 1:
                        split_to(u0 + 3 * j + 4)
                    product(j, j % 2)
                    if j < NJ - 1:
                        split_to(u0 + 3 * j + 5)
                    gate_lo(j, j % 2)
                    if j == NJ - 1:
                        split_to(u0 + 3 * NJ)

                for j in range(3):
                    chunk(j)
                    if layer == 0 and j == 1:
                        dve.wait_ge(consts_act, 3)
                        V.tensor_tensor(wf_lo, wf_sb, wf_hi.bitcast(F32), ALU.subtract).then_inc(consts_dve, 1)
                with dve.Fori(0, (NJ - 5) // 2) as i:
                    for par in range(2):
                        j = 2 * i + (3 + par)

                        def split(k):
                            first = u0 + 3 * (3 + par) + k
                            split_lo(first + 6 * i, first % HL, first % RAW)

                        split(2)
                        scaled(j, e0 + 3 + par, u0 + 3 * j + 1)
                        taps(j, (3 + par) % 2)
                        split(3)
                        product(j, (3 + par) % 2)
                        split(4)
                        gate_lo(j, (3 + par) % 2)
                nsplit[0] = u0 + 3 * (NJ - 2) + 2
                for j in (NJ - 2, NJ - 1):
                    chunk(j)

            def stick():
                s = sz
                for i in range(H + 6):
                    if 8 <= i < 12:
                        split_quarter(U0["sb_o"] + 2, i - 8)
                    if i < H:
                        if i % 2:
                            dve.wait_ge(s["logit"], i + 1)
                            if i >= 2:
                                dve.wait_ge(s["exp"], i - 1)
                            magnitude(st_abs[i % 2], stick_bank(i)[:, 0:384]).then_inc(s["abs_odd"], 1)
                    if 0 <= i - 1 < H:
                        j = i - 1
                        dve.wait_ge(s["ln"], j + 1)
                        if j >= 3:
                            dve.wait_ge(s["later"], j - 2)
                        kp, hi, lo = (b[j % 3] for b in (st_keep, st_khi, st_klo))
                        V.scalar_tensor_tensor(kp, stick_bank(j)[:, 0:384], 0.0, st_exp[j % 2], ALU.max, ALU.add).then_inc(s["keep"], 1)
                        dve.wait_ge(s["keep"], j + 1)
                        settle(V.tensor_copy(hi, kp))
                        V.tensor_tensor(lo, kp, hi.bitcast(F32), ALU.subtract).then_inc(s["split"], 1)
                    if i >= 6 and i % 2 == 0 and (i - 6) // 2 * 2 + 1 < H:
                        p = (i - 6) // 2
                        dve.wait_ge(s["ohi"], p + 1)
                        V.tensor_tensor(oT_lo[:, p, :], psC[:, p % 2, 0:T], oT_hi[:, p, :].bitcast(F32),
                                        ALU.subtract).then_inc(s["olo"], 1)

            def softmax_attn(w):
                s = sm[w]
                for i in range(H + 6):
                    if 8 <= i < 12:
                        split_quarter(U0[("fox_o", "at_o")[w]] + 2, i - 8)
                    if i < H:
                        dve.wait_ge(s["logit"], i + 1)
                        V.tensor_reduce(mx[:, w, i, 0:1], psD[:, i % 4, 0:P], AX.X, ALU.max)
                        settle(V.tensor_reduce(mx[:, w, i, 1:2], psD[:, i % 4, P:384], AX.X, ALU.max))
                        if w:
                            V.tensor_scalar(nmx[:, w, i, :], mx[:, w, i, :], sink_bc[:, i:i + 1], -1.0, ALU.max,
                                            ALU.mult).then_inc(s["max"], 1)
                        else:
                            V.tensor_scalar(nmx[:, w, i, :], mx[:, w, i, :], -1.0, None, ALU.mult).then_inc(s["max"], 1)
                    if 0 <= i - 1 < H:
                        j = i - 1
                        dve.wait_ge(s["exp"], j + 1)
                        if w:
                            settle(V.tensor_tensor(sums[:, w, j, :], sums[:, w, j, :], esink[:, j, :], ALU.add))
                        settle(V.reciprocal(rsum[:, w, j, :], sums[:, w, j, :]))
                        V.tensor_scalar(sm_p[j % 5][:, 0:P], sm_p[j % 5][:, 0:P], rsum[:, w, j, 0:1], None, ALU.mult)
                        V.tensor_scalar(sm_p[j % 5][:, P:384], sm_p[j % 5][:, P:384], rsum[:, w, j, 1:2], None,
                                        ALU.mult).then_inc(s["norm"], 1)
                    if i >= 6 and i % 2 == 0 and (i - 6) // 2 * 2 + 1 < H:
                        p = (i - 6) // 2
                        src = psC[:, p % 2, 0:T]
                        if w:
                            dve.wait_ge(s["out"], 2 * p + 2)
                            V.tensor_tensor(gated_t[:, p % 2, :], src, zT[:, p, :], ALU.mult).then_inc(s["gated"], 1)
                            src = gated_t[:, p % 2, :]
                        dve.wait_ge(s["ohi"], p + 1)
                        V.tensor_tensor(oT_lo[:, p, :], src, oT_hi[:, p, :].bitcast(F32), ALU.subtract).then_inc(s["olo"], 1)

            V.memset(ones_row[:, :], 1.0)
            V.memset(eps_t[:, :], EPS).then_inc(consts_dve, 1)
            dve.wait_ge(pv_loaded, 16)
            pre(0, "sb_pre")
            split_to(2)
            pre_scales(0)
            split_to(3)

            dve.wait_ge(small_loaded, 16 * 7)
            settle(V.tensor_copy(pos_f[:, :], pos_i[:, :]))
            inv_freq = np.float32(ROPE_THETA) ** (-(np.arange(ROPE_HALF, dtype=np.float32) * np.float32(2.0) / np.float32(2 * ROPE_HALF)))
            for d in range(ROPE_HALF):
                ins = V.tensor_scalar(ang[:, 0, :, d], pos_f[:, :], float(np.float32(inv_freq[d])), None, ALU.mult)
            settle(ins)
            MAGIC = 1.5 * 2.0 ** 23
            settle(V.tensor_scalar(ang[:, 1, :, :], ang[:, 0, :, :], float(1.0 / (2 * np.pi)), MAGIC, ALU.mult, ALU.add))
            settle(V.tensor_scalar(ang[:, 1, :, :], ang[:, 1, :, :], MAGIC, None, ALU.subtract))
            two_pi = 2 * np.pi
            c1 = 6.28125
            c2 = float(np.float32(np.round((two_pi - c1) * 2.0 ** 20) / 2.0 ** 20))
            c3 = float(np.float32(two_pi - c1 - c2))
            for piece in (c1, c2, c3):
                settle(V.scalar_tensor_tensor(ang[:, 0, :, :], ang[:, 1, :, :], -piece, ang[:, 0, :, :], ALU.mult, ALU.add))
            settle(V.tensor_scalar(ang[:, 2, :, :], ang[:, 0, :, :], 3.1415925, -3.1415925, ALU.min, ALU.max))
            settle(magnitude(ang[:, 1, :, :], ang[:, 2, :, :]))
            V.tensor_scalar(ang[:, 3, :, :], ang[:, 1, :, :], -1.0, float(np.float32(np.pi / 2)), ALU.mult,
                            ALU.add).then_inc(rope["arg"], 1)
            split_to(4)
            pre_spread(0)
            for c in range(4):
                split_to(U0["sb_qk"] + 2 * c + 4)
                if c < 2:
                    evac_features("sb_qk", c, qT, QSCALE)
                else:
                    evac_features("sb_qk", c, kT, first=2)
            for c in range(2):
                split_to(U0["sb_v"] + 2 * c + 4)
                evac("sb_v", c, vt[:, 0, 512 * c:512 * c + 512], 0)
            stick()
            split_to(U0["ffn0"] + 1)
            post(0)
            pre(1, "ffn_pre0")
            split_to(U0["ffn0"] + 2)
            pre_scales(1)
            split_to(U0["ffn0"] + 4)
            pre_spread(1)
            conv_ffn(0)
            split_to(U0["fox_k"] + 1)
            post(1)
            pre(2, "kv")
            split_to(U0["fox_k"] + 2)
            pre_scales(2)
            split_to(U0["fox_k"] + 3)
            pre_spread(2)
            split_to(U0["fox_k"] + 4)
            evac_features("fox_k", 0, kT)
            split_to(U0["fox_k"] + 5)
            for k in range(KT):
                dve.wait_ge(xT_hi_done, xt_base(2) + 4 + k + 1)
                V.scalar_tensor_tensor(oT_lo[:, k, :], hn_T[:, k, :], col("fox_pre", k), oT_hi[:, k, :].bitcast(F32),
                                       ALU.mult, ALU.subtract).then_inc(xT_lo_done, 1)
            dve.wait_ge(forget["product"], 1)
            settle(V.tensor_tensor(ftmp[:, 0, :], psD[0:F2, 1, 0:T], scale_row[0:F2, :], ALU.mult))
            settle(V.tensor_scalar(ftmp[:, 0, :], ftmp[:, 0, :], bf_sb[:, :], None, ALU.add))
            magnitude(ftmp[:, 1, :], ftmp[:, 0, :]).then_inc(forget["bias"], 1)
            split_to(U0["fox_k"] + 6)
            evac_features("fox_k", 1, kT)
            dve.wait_ge(forget["ln"], 1)
            settle(V.scalar_tensor_tensor(ftmp[:, 2, :], ftmp[:, 0, :], 0.0, ftmp[:, 1, :], ALU.min, ALU.subtract))
            settle(V.tensor_tensor_scan(ftmp[:, 1, :], ones_row[0:F2, :], ftmp[:, 2, :], 0.0, ALU.mult, ALU.add))
            for c in range(2):
                split_to(U0["fox_v"] + 2 * c + 4)
                evac("fox_v", c, vt[:, 0, 512 * c:512 * c + 512], 2)
            dve.wait_ge(consts_pool, N_CONSTS)
            settle(V.tensor_scalar(neg_f, ones_row[:, :], 0.0, None, ALU.mult))
            settle(V.tensor_scalar(neg_f[0:F2], ftmp[:, 1, :], -1.0, None, ALU.mult))
            V.scalar_tensor_tensor(neg_f[32:F2], ftmp[32:F2, 1, :], -1.0, neg_f[32:F2].bitcast(F32), ALU.mult, ALU.subtract)
            V.tensor_copy(sel_r, sel).then_inc(forget["cum"], 1)
            for c in range(2):
                split_to(U0["fox_q"] + 2 * c + 4)
                evac_features("fox_q", c, qT, QSCALE)
            softmax_attn(0)
            split_to(U0["ffn1"] + 1)
            post(2)
            pre(3, "ffn_pre1")
            split_to(U0["ffn1"] + 2)
            pre_scales(3)
            split_to(U0["ffn1"] + 4)
            pre_spread(3)
            conv_ffn(1)
            split_to(U0["at_q"] + 1)
            post(3)
            pre(4, "at_pre")
            split_to(U0["at_q"] + 2)
            pre_scales(4)
            split_to(U0["at_q"] + 3)
            pre_spread(4)
            dve.wait_ge(bias_loaded, 32)
            for c in range(2):
                split_to(U0["at_q"] + 2 * c + 4)
                chunk_wait("at_q", c)
                for tt in range(TT):
                    ins = V.scalar_tensor_tensor(qk_tok[:, tt, 512 * c:512 * c + 512], bank(E0["at_q"] + c, tt),
                                                 st[:, 8, 4, tt:tt + 1], bin_bc[:, 512 * c:512 * c + 512], ALU.mult, ALU.add)
                ins.then_inc(chunk_freed_v, 1)
            split_to(U0["at_kv"] + 3)
            dve.wait_ge(unit_done, U0["at_kv"] + 1)
            for tt in range(TT):
                kv, r = bank(E0["at_kv"], tt), st[:, 8, 4, tt:tt + 1]
                V.scalar_tensor_tensor(qk_tok[:, tt, D:D + KVW], kv[:, 0:KVW], r, bin_bc[:, D:D + KVW], ALU.mult, ALU.add)
                ins = V.scalar_tensor_tensor(vt[:, tt, 0:KVW], kv[:, KVW:2 * KVW], r, bin_bc[:, D + KVW:D + 2 * KVW],
                                             ALU.mult, ALU.add)
            ins.then_inc(chunk_freed_v, 1)
            dve.wait_ge(chunk_freed_v, V_FREED[E0["at_kv"]])
            dve.wait_ge(rope["sin"], 1)
            heads = qk_tok.rearrange("p t (h d) -> p t h d", d=DH)
            for tt in range(TT):
                hd = heads[:, tt]
                sin_, cos_ = (cosin[:, i, tt:tt + 1, :].to_broadcast([P, H + 2, ROPE_HALF]) for i in range(2))
                x1, x2 = hd[:, :, 0:ROPE_HALF], hd[:, :, ROPE_HALF:2 * ROPE_HALF]
                t = [rtmp[:, i, 18 * tt:18 * tt + 18, :] for i in range(4)]
                V.tensor_tensor(t[0], x1, cos_, ALU.mult)
                V.tensor_tensor(t[1], x2, sin_, ALU.mult)
                V.tensor_tensor(t[2], x2, cos_, ALU.mult)
                settle(V.tensor_tensor(t[3], x1, sin_, ALU.mult))
                V.tensor_tensor(x1, t[0], t[1], ALU.subtract)
                settle(V.tensor_tensor(x2, t[2], t[3], ALU.add))
            keys = qk_tok[:, :, D:D + KVW].rearrange("p t (g d) -> p t g d", g=2)
            V.tensor_copy(kdup[:, :, :, 0, :], keys)
            V.tensor_copy(kdup[:, :, :, 1, :], keys).then_inc(rope["applied"], 1)
            split_to(U0["at_z"] + 4)
            evac_features("at_z", 0, zT, None, rope["z"])
            split_to(U0["at_z"] + 5)
            dve.wait_ge(rope["q_turned"], 1)
            for b in range(4):
                ins = V.tensor_scalar(qT[:, 2 * b:2 * b + 2, :].rearrange("p k t -> p (k t)"), psD[:, b, :], QSCALE, None, ALU.mult)
            ins.then_inc(rope["q_copied"], 1)
            dve.wait_ge(rope["k_turned"], 1)
            V.tensor_copy(kT[:, 0:2, :].rearrange("p k t -> p (k t)"), psD[:, 0, :]).then_inc(rope["k_copied"], 1)
            split_to(U0["at_z"] + 6)
            evac_features("at_z", 1, zT, None, rope["z"])
            softmax_attn(1)
            split_to(U0["rec_f"] + 1)
            post(4)
            pre(5, "rec_pre")
            split_to(U0["rec_f"] + 2)
            pre_scales(5)
            split_to(U0["rec_f"] + 3)
            pre_spread(5)

            settle(V.tensor_tensor(lbv[:, 0, :], col("lb1", 0, 8), col("lb0", 0, 8), ALU.subtract))
            magnitude(lbv[:, 1, :], lbv[:, 0, :]).then_inc(rec["v1"], 1)
            dve.wait_ge(rec["s1"], 1)
            settle(V.scalar_tensor_tensor(lbv[:, 2, :], lbv[:, 0, :], 0.0, lbv[:, 1, :], ALU.min, ALU.subtract))
            settle(V.tensor_tensor(lbv[:, 3, :], lbv[:, 2, :], lbv[:, 0, :], ALU.subtract))
            settle(V.tensor_scalar(lbv[:, 4, :], lbv[:, 0, :], -1.0, None, ALU.mult))

            def head(ap, k):
                return ap[:, T * k:T * k + T]

            for c in range(2):
                split_to(U0["rec_f"] + 2 * c + 4)
                evac_features("rec_f", c, kT)
            dve.wait_ge(chunk_freed_v, V_FREED[E0["rec_f"] + 1])
            magnitude(X[0], LV).then_inc(rec["v1"], 1)
            split_to(U0["rec_q"] + 3)
            dve.wait_ge(rec["s1"], 2)
            settle(V.scalar_tensor_tensor(kk, LV, 0.0, X[0], ALU.min, ALU.subtract))
            for k in range(KT):
                ins = V.tensor_scalar(head(cum, k), head(kk, k), lbv[:, 4, k:k + 1], None, ALU.add)
            settle(ins)
            magnitude(X[1], cum).then_inc(rec["v1"], 1)
            split_to(U0["rec_q"] + 4)
            evac_features("rec_q", 0, qT)
            split_to(U0["rec_q"] + 5)
            for k in range(KT):
                ins = V.tensor_scalar(head(X[0], k), head(kk, k), lbv[:, 3, k:k + 1], lbv[:, 2, k:k + 1], ALU.add, ALU.max)
            ins.then_inc(rec["v1"], 1)
            dve.wait_ge(rec["v1"], 4)
            split_to(U0["rec_q"] + 6)
            dve.wait_ge(rec["s1"], 3)
            settle(V.tensor_tensor(X[0], X[0], X[1], ALU.add))
            split_to(U0["rec_q"] + 7)
            evac_features("rec_q", 1, qT)
            for g in range(TT * REC_H):
                ins = V.tensor_tensor_scan(cum[:, P * g:P * g + P], ones_row[:, 0:P], X[0][:, P * g:P * g + P], 0.0,
                                           ALU.mult, ALU.add)
            settle(ins)
            dve.wait_ge(rec["s1"], 4)
            dve.wait_ge(rec["cleared"], 1)
            V.memset(st[:, 0, 3, :], 0.0).then_inc(rec["ready"], 1)
            q_all = qT[:, :, :].rearrange("p k t -> p (k t)")

            def query_diff(li):
                m = LEVELS[li]
                c4, l4 = level_view(cum, m), level_view(LV, m)
                if li >= 1:
                    dve.wait_ge(rec["qx"], li)
                    dve.wait_ge(rec["kx"], li)
                if m == P:
                    V.memset(st[:, 0, 3, :], 0.0).then_inc(rec["qdiff"], 1)
                else:
                    ref = c4[:, :, 0, m - 1:m].to_broadcast([P, T * REC_H // (2 * m), m])
                    V.tensor_tensor(l4[:, :, 1, :], c4[:, :, 1, :], ref, ALU.subtract).then_inc(rec["qdiff"], 1)

            def query_side(li):
                m = LEVELS[li]
                dve.wait_ge(rec["qexp"], li + 1)
                if li >= 2:
                    dve.wait_ge(rec["level"], 2 * li)
                l4, x4, q4 = (level_view(a, m) for a in (LV, X[li % 2], q_all))
                V.tensor_tensor(x4[:, :, 1, :], l4[:, :, 1, :], q4[:, :, 1, :], ALU.mult).then_inc(rec["qx"], 1)

            def pick(n):
                for half in range(2):
                    dve.wait_ge(rec["level"], 2 * n + half + 1)
                    if n or half:
                        dve.wait_ge(rec["picked"], 2 * n + half)
                    V.copy_predicated(sc_diag[:, 1024 * half:1024 * half + 1024].rearrange("p (g t) -> p g t", t=P),
                                      mask_level[:, n, :].unsqueeze(1).to_broadcast([P, 8, P]),
                                      psD_rows[:, half, :].rearrange("p (g t) -> p g t", t=P)).then_inc(rec["picked"], 1)

            def level_step(li):
                query_diff(li)
                if li:
                    pick(li - 1)
                if li == 0:
                    dve.wait_ge(rec["silu"], 1)
                query_side(li)

            for i, (name, c, dst) in enumerate((("rec_z", 0, hn[:, 0, 0:512]), ("rec_z", 1, hn[:, 0, 512:1024]),
                                                ("rec_i", 0, vt[:, 0, 0:512]), ("rec_i", 1, vt[:, 0, 512:1024]))):
                u = U0[name] + 2 * c
                split_to(u + 3)
                if i:
                    level_step(2 * i - 1)
                split_to(u + 4)
                level_step(2 * i)
                evac(name, c, dst, 5)
            level_step(7)
            pick(7)
            dve.wait_ge(rec["cross"], 1)
            V.tensor_copy(sc_cross, psC[:, 0:2, :].rearrange("p b n -> p (b n)")).then_inc(rec["crossed"], 1)
            dve.wait_ge(rec["silu"], 2)
            gate = hn[:, :, :].rearrange("p t (h v) -> p (t h) v", v=P)
            settle(V.tensor_tensor(gate, gate, gn_bc[:, :].unsqueeze(1).to_broadcast([P, TT * REC_H, P]), ALU.mult))
            for tt in range(TT):
                r = slice(tt * REC_H, tt * REC_H + REC_H)
                for b in range(2):
                    dve.wait_ge(rec["osq"], 2 * tt + b + 1)
                    V.tensor_tensor(X[1][:, tt * D + 512 * b:tt * D + 512 * b + 512], psD[:, 2 * tt + b, :],
                                    hn[:, tt, 512 * b:512 * b + 512], ALU.mult)
                settle(V.tensor_scalar(rst[:, 3, r], rst[:, 0, r], 1.0 / P, EPS, ALU.mult, ALU.add))
                dve.wait_ge(rec["oguess"], tt + 1)
                V.tensor_scalar(rst[:, 5, r], rst[:, 2, r], -0.5, None, ALU.mult)
                settle(V.tensor_tensor(rst[:, 4, r], rst[:, 2, r], rst[:, 2, r], ALU.mult))
                settle(V.tensor_tensor(rst[:, 4, r], rst[:, 4, r], rst[:, 3, r], ALU.mult))
                settle(V.scalar_tensor_tensor(rst[:, 5, r], rst[:, 4, r], 3.0, rst[:, 5, r], ALU.subtract, ALU.mult))
                og = X[1][:, tt * D:tt * D + D].rearrange("p (h v) -> p h v", v=P)
                for b in range(2):
                    half = og[:, 4 * b:4 * b + 4]
                    V.tensor_tensor(half, half, rst[:, 5, tt * REC_H + 4 * b:tt * REC_H + 4 * b + 4].unsqueeze(2).to_broadcast([P, 4, P]),
                                    ALU.mult).then_inc(rec["gated"], 1)
            for b in range(4):
                dve.wait_ge(rec["ohi"], b + 1)
                dst = oT_lo[:, 2 * b:2 * b + 2, :].rearrange("p k t -> p (k t)")
                V.tensor_tensor(dst, psC[:, b, :], oT_hi[:, 2 * b:2 * b + 2, :].rearrange("p k t -> p (k t)").bitcast(F32),
                                ALU.subtract).then_inc(rec["olo"], 1)
            split_to(NU)
            post(5)

        @block.tensor
        def _(pe):
            MM = nc.tensor.matmul

            def product3(out, lhs, rhs, start, stop):
                MM(out, lhs[0], rhs[0], start=start, stop=False, skip_group_check=True)
                MM(out, lhs[0], rhs[1], start=False, stop=False, skip_group_check=True)
                return MM(out, lhs[1], rhs[0], start=False, stop=stop, skip_group_check=True)

            def stay_warm(out, count, constant):
                for _ in range(count):
                    MM(out, constant[:, :], constant[:, :], start=True, stop=True, skip_group_check=True)

            def turn(n):
                if n == 0:
                    pe.wait_ge(ident_made, 1)
                for tt in range(TT):
                    if n and tt:
                        stay_warm(psC[:, xbank(n, 3), T + P:2 * T], 16, neg_tri_r)
                    for k in range(KT):
                        if n == 0 and k == 0:
                            pe.wait_ge(x_loaded[tt], 16)
                        if n and k % 4 == 0:
                            pe.wait_ge(h_new, 2 * (TT * (n - 1) + tt) + k // 4 + 1)
                        at = (k % 2) * T + tt * P
                        nc.tensor.transpose(psC[:, xbank(n, k // 2), at:at + P], h[:, tt, k * P:k * P + P], ident[:, :]).then_inc(xT_turned, 1)
                if n:
                    stay_warm(psD[:, 3, 0:P], 17, neg_tri_r)
                else:
                    stay_warm(psD[:, 3, 0:P], 14, ident)

            def spread_scales(n):
                pe.wait_ge(diag_made, TT * (n + 1))
                if n == 0:
                    pe.wait_ge(ones_made, 1)
                MM(psD[:, 0, 0:T], neg_ones[:, :], scale_diag[:, :], start=True, stop=True).then_inc(scale_spread, 1)

            def x_wait(n, half):
                pe.wait_ge(xT_lo_done, xt_base(n) + 2 * half + 2)

            def wait_banks(e):
                if e >= 2:
                    pe.wait_ge(chunk_freed_v, V_FREED[e - 2])
                    pe.wait_ge(chunk_freed_s, S_FREED[e - 2])

            def features_half(u, uslot, e, half, xt):
                hi = w_hi[:, uslot, :].rearrange("p (k n) -> p k n", k=4)
                lo = w_lo[:, uslot, :].rearrange("p (k n) -> p k n", k=4)
                pe.wait_ge(lo_done, u + 1)
                for a in range(4):
                    out = psC[:, 2 * (e % 2) + a // 2, (a % 2) * T:(a % 2) * T + T]
                    for k in range(4):
                        kk_ = 4 * half + k
                        ins = product3(out, (hi[:, k, a * P:a * P + P], lo[:, k, a * P:a * P + P]),
                                       (xt[0][:, kk_, :], xt[1][:, kk_, :]), start=(kk_ == 0 and a % 2 == 0),
                                       stop=(kk_ == KT - 1))
                ins.then_inc(unit_done, 1)

            def features(name, n, xt, pre_n=None):
                for c in range(n):
                    e = E0[name] + c
                    wait_banks(e)
                    for half in range(2):
                        u = U0[name] + 2 * c + half
                        if pre_n is not None and c == 0:
                            x_wait(pre_n, half)
                        features_half(u, u % HL, e, half, xt)
                    if pre_n is not None and c == 0:
                        spread_scales(pre_n)

            def tokens_half(u, outs, half, xt):
                hi = unit_hi(u).rearrange("p (k n) -> p k n", k=4)
                lo = unit_lo(u).rearrange("p (k n) -> p k n", k=4)
                pe.wait_ge(lo_done, u + 1)
                for tt in range(TT):
                    for k in range(4):
                        kk_ = 4 * half + k
                        ins = product3(outs[tt], (xt[0][:, kk_, tt * P:tt * P + P], xt[1][:, kk_, tt * P:tt * P + P]),
                                       (hi[:, k, :], lo[:, k, :]), start=(kk_ == 0), stop=(kk_ == KT - 1))
                ins.then_inc(unit_done, 1)

            def tokens(name, n, xt, pre_n=None):
                for c in range(n):
                    e = E0[name] + c
                    wait_banks(e)
                    for half in range(2):
                        if pre_n is not None and c == 0:
                            x_wait(pre_n, half)
                        tokens_half(U0[name] + 2 * c + half, [bank(e, tt) for tt in range(TT)], half, xt)
                    if pre_n is not None and c == 0:
                        spread_scales(pre_n)

            def gather(name, xt, lo_parts, per_half):
                u = U0[name]
                for half in range(2):
                    pe.wait_ge(lo_parts, per_half * (half + 1))
                    tokens_half(u + half, [psD[:, 2 * tt, :] for tt in range(TT)], half, xt)
                parts = [[a(u + 2 + half).rearrange("p (k n) -> p k n", k=4) for a in (unit_hi, unit_lo)] for half in range(2)]
                for tt in range(TT):
                    for half in range(2):
                        if tt == 0:
                            pe.wait_ge(lo_done, u + 2 + half + 1)
                        hi, lo = parts[half]
                        for k in range(4):
                            kk_ = 4 * half + k
                            ins = product3(psD[:, 2 * tt + 1, :], (xt[0][:, kk_, tt * P:tt * P + P], xt[1][:, kk_, tt * P:tt * P + P]),
                                           (hi[:, k, :], lo[:, k, :]), start=(kk_ == 0), stop=(kk_ == KT - 1))
                        if tt:
                            ins.then_inc(unit_done, 1)
                        elif half:
                            ins.then_inc(rows_done, 1)

            def conv_ffn(layer):
                f, u0, e0 = ffn[layer], U0[f"ffn{layer}"], E0[f"ffn{layer}"]
                xt = (xT_hi, xT_lo)
                pre_n = 1 + 2 * layer

                def down(d, u, uslot, par, first, last):
                    hi = w_hi[:, uslot, :].rearrange("p (k n) -> p k n", k=2)
                    lo = w_lo[:, uslot, :].rearrange("p (k n) -> p k n", k=2)
                    pe.wait_ge(lo_done, u + 1)
                    pe.wait_ge(f["g_lo"], d + 1)
                    for tt in range(TT):
                        for c in range(2):
                            for k in range(2):
                                ins = product3(psD[:, 2 * tt + c, :],
                                               (gT_hi[:, par, k, tt * P:tt * P + P], gT_lo[:, par, k, tt * P:tt * P + P]),
                                               (hi[:, k, 512 * c:512 * c + 512], lo[:, k, 512 * c:512 * c + 512]),
                                               start=(first and k == 0), stop=(last and k == 1))
                            if last and (tt, c) != (1, 1):
                                ins.then_inc(rows_done, 1)
                    ins.then_inc(unit_done, 1)

                def up(j, u):
                    e = e0 + j
                    if j >= 2:
                        pe.wait_ge(f["scaled"], 2 * (j - 1))
                    else:
                        wait_banks(e)
                    for half in range(2):
                        if j == 0:
                            x_wait(pre_n, half)
                        features_half(u + half, (u + half) % HL, e, half, xt)
                    if j == 0:
                        spread_scales(pre_n)

                def down_peeled(j, u):
                    down(j, u, u % HL, j % 2, j == 0, j == NJ - 1)

                up(0, u0)
                for j in range(1, 3):
                    up(j, u0 + 3 * j - 1)
                    down_peeled(j - 1, u0 + 3 * j + 1)
                with pe.Fori(0, (NJ - 5) // 2) as i:
                    for par in range(2):
                        j0 = 3 + par
                        first = u0 + 3 * j0 - 1
                        pe.wait_ge(f["scaled"], 4 * i + 2 * (j0 - 1))
                        for half in range(2):
                            features_half(first + half + 6 * i, (first + half) % HL, e0 + j0, half, xt)
                        down(2 * i + (j0 - 1), first + 2 + 6 * i, (first + 2) % HL, (j0 - 1) % 2, False, False)
                u = u0 + 3 * NJ - 7
                up(NJ - 2, u)
                up(NJ - 1, u + 2)
                for i in range(3):
                    down_peeled(NJ - 3 + i, u + 4 + i)

            def stick():
                s = sz
                pe.wait_ge(consts_pool, N_CONSTS)
                pe.wait_ge(consts_act, 2)
                pe.wait_ge(chunk_freed_v, V_FREED[E0["sb_v"] + 1])
                pe.wait_ge(chunk_freed_s, S_FREED[E0["sb_v"] + 1])
                for i in range(H + 5):
                    if i < H:
                        p0, k = DH * (i % 2), i // 2
                        if i >= 6:
                            pe.wait_ge(s["prob"], i - 5)
                        z = stick_bank(i)
                        MM(z[:, 0:384], ident_b[:, :], mask_stick[:, :], start=True, stop=False, skip_group_check=True)
                        MM(z[:, 0:T], kT[p0:p0 + DH, k, 0:P], qT[p0:p0 + DH, k, :], start=False, stop=False, skip_group_check=True)
                        MM(z[:, T:384], kT[p0:p0 + DH, k, P:T], qT[p0:p0 + DH, k, P:T], start=False, stop=False,
                           skip_group_check=True).then_inc(s["logit"], 1)
                    if 0 <= i - 4 < H:
                        j = i - 4
                        pe.wait_ge(s["split"], j + 1)
                        z = stick_bank(j)
                        for part in (st_khi[j % 3], st_klo[j % 3]):
                            MM(z[:, 0:384], neg_tri_r[:, :], part, start=False, stop=False, skip_group_check=True)
                            ins = MM(z[:, P:T], neg_ones_r[:, :], part[:, T:384], start=False, stop=(part is not st_khi[j % 3]),
                                     skip_group_check=True)
                        ins.then_inc(s["later"], 1)
                    if 0 <= i - 5 < H:
                        j = i - 5
                        pe.wait_ge(s["prob"], j + 1)
                        if j % 2 == 0 and j >= 4:
                            pe.wait_ge(s["olo"], j // 2 - 1)
                        value(j, st_prob[j % 3], j * DH).then_inc(s["out"], 1)

            def value(j, probT, vcol):
                p0 = DH * (j % 2)
                o = psC[p0:p0 + DH, (j // 2) % 2, 0:T]
                MM(o, vt[:, 0, vcol:vcol + DH], probT[:, 0:T], start=True, stop=False, skip_group_check=True)
                return MM(o[:, P:T], vt[:, 1, vcol:vcol + DH], probT[:, T:384], start=False, stop=True, skip_group_check=True)

            def softmax_attn(w):
                s = sm[w]
                for i in range(H + 6):
                    if i < H:
                        p0, k = DH * (i % 2), i // 2
                        kk_ = i // 8 if w else k
                        if i >= 4:
                            pe.wait_ge(s["exp"], i - 3)
                        z = psD[:, i % 4, :]
                        MM(z[:, 0:384], ident_b[:, :], (mask_window if w else mask_causal)[:, :], start=True, stop=False,
                           skip_group_check=True)
                        if not w:
                            MM(z[:, 0:P], sel_r[:, i, :], neg_f[:, 0:P], start=False, stop=False, skip_group_check=True)
                            MM(z[:, P:384], sel_r[:, i, :], neg_f, start=False, stop=False, skip_group_check=True)
                        MM(z[:, 0:P], qT[p0:p0 + DH, k, 0:P], kT[p0:p0 + DH, kk_, 0:P], start=False, stop=False, skip_group_check=True)
                        MM(z[:, P:384], qT[p0:p0 + DH, k, P:T], kT[p0:p0 + DH, kk_, :], start=False, stop=True,
                           skip_group_check=True).then_inc(s["logit"], 1)
                    if 0 <= i - 4 < H:
                        j = i - 4
                        pe.wait_ge(s["norm"], j + 1)
                        if w and j == 0:
                            pe.wait_ge(chunk_freed_v, V_FREED[E0["at_z"] + 1])
                        if j >= 2:
                            pe.wait_ge(s["pT"], j - 1)
                        for b in range(3):
                            ins = nc.tensor.transpose(psC[:, 2 + j % 2, P * b:P * b + P], sm_p[j % 5][:, P * b:P * b + P], ident[:, :])
                        ins.then_inc(s["turned"], 1)
                    if 0 <= i - 5 < H:
                        j = i - 5
                        pe.wait_ge(s["pT"], j + 1)
                        if j % 2 == 0 and j >= 4:
                            pe.wait_ge(s["olo"], j // 2 - 1)
                        value(j, sm_pT[j % 3], (j // 8 if w else j) * DH).then_inc(s["out"], 1)

            xt = (xT_hi, xT_lo)
            ot = (oT_hi, oT_lo)
            turn(0)
            features("sb_qk", 4, xt, 0)
            tokens("sb_v", 2, xt)
            stick()
            gather("sb_o", ot, sz["olo"], H // 4)
            turn(1)
            conv_ffn(0)
            turn(2)
            pe.wait_ge(consts_dve, 2)
            for half in range(2):
                x_wait(2, half)
                for k in range(4 * half, 4 * half + 4):
                    ins = product3(psD[0:F2, 1, 0:T], (wf_hi[:, k, :], wf_lo[:, k, :]), (xT_hi[:, k, :], xT_lo[:, k, :]),
                                   start=(k == 0), stop=(k == KT - 1))
            ins.then_inc(forget["product"], 1)
            pe.wait_ge(raw_kept, 4)
            features("fox_k", 2, xt, 2)
            tokens("fox_v", 2, xt)
            pe.wait_ge(xT_lo_done, xt_base(3))
            features("fox_q", 2, ot)
            pe.wait_ge(chunk_freed_v, V_FREED[E0["fox_q"] + 1])
            pe.wait_ge(chunk_freed_s, S_FREED[E0["fox_q"] + 1])
            pe.wait_ge(forget["cum"], 1)
            softmax_attn(0)
            gather("fox_o", ot, sm[0]["olo"], H // 4)
            turn(3)
            conv_ffn(1)
            turn(4)
            tokens("at_q", 2, xt, 4)
            e, u = E0["at_kv"], U0["at_kv"]
            wait_banks(e)
            pe.wait_ge(lo_done, u + 1)
            hi8, lo8 = (a.rearrange("p (k n) -> p k n", k=KT) for a in (unit_hi(u), unit_lo(u)))
            for tt in range(TT):
                for k in range(KT):
                    ins = product3(bank(e, tt)[:, 0:256], (xT_hi[:, k, tt * P:tt * P + P], xT_lo[:, k, tt * P:tt * P + P]),
                                   (hi8[:, k, :], lo8[:, k, :]), start=(k == 0), stop=(k == KT - 1))
            ins.then_inc(unit_done, 1)
            features("at_z", 1, xt)
            pe.wait_ge(rope["applied"], 1)
            pe.wait_ge(chunk_freed_v, V_FREED[E0["at_kv"]])
            for k in range(KT):
                for tt in range(TT):
                    at = (k % 2) * T + tt * P
                    ins = nc.tensor.transpose(psD[:, k // 2, at:at + P], qk_tok[:, tt, k * P:k * P + P], ident[:, :])
            ins.then_inc(rope["q_turned"], 1)
            e, u = E0["at_z"] + 1, U0["at_z"] + 2
            wait_banks(e)
            features_half(u, u % HL, e, 0, xt)
            pe.wait_ge(rope["q_copied"], 1)
            for g in range(2):
                for tt in range(TT):
                    at = g * T + tt * P
                    ins = nc.tensor.transpose(psD[:, 0, at:at + P], kdup[:, tt, g, :, :].rearrange("p r d -> p (r d)"), ident[:, :])
            ins.then_inc(rope["k_turned"], 1)
            features_half(u + 1, (u + 1) % HL, e, 1, xt)
            pe.wait_ge(rope["k_copied"], 1)
            softmax_attn(1)
            gather("at_o", ot, sm[1]["olo"], H // 4)
            turn(5)
            features("rec_f", 2, xt, 5)
            features("rec_q", 2, xt)

            def level(n):
                for half in range(2):
                    if n:
                        pe.wait_ge(rec["kx"], n)
                        pe.wait_ge(rec["qx"], n)
                        pe.wait_ge(rec["picked"], 2 * (n - 1) + half + 1)
                    for g in range(8):
                        tile = 8 * half + g
                        if n:
                            a = b = X[(n - 1) % 2][:, P * tile:P * tile + P]
                        else:
                            a = kk[:, P * tile:P * tile + P]
                            b = qT[:, tile // 2, P * (tile % 2):P * (tile % 2) + P]
                        ins = MM(psD[:, 2 * half + g // 4, P * (g % 4):P * (g % 4) + P], a, b, start=(g % 4 == 0), stop=True,
                                 skip_group_check=True)
                    ins.then_inc(rec["level"], 1)

            for i, (name, c) in enumerate((("rec_z", 0), ("rec_z", 1), ("rec_i", 0), ("rec_i", 1))):
                e = E0[name] + c
                wait_banks(e)
                for half in range(2):
                    tokens_half(U0[name] + 2 * c + half, [bank(e, tt) for tt in range(TT)], half, xt)
                    if i == 1 and half == 0:
                        pe.wait_ge(rec["ready"], 1)
                        pe.wait_ge(rec["silu"], 1)
                    if 2 * i + half >= 2:
                        level(2 * i + half - 2)
            level(6)
            level(7)

            def outputs(tt):
                for g in range(REC_H):
                    o = psD[:, 2 * tt + g // 4, P * (g % 4):P * (g % 4) + P]
                    s_tile = 2 * g + tt
                    ins = MM(o, sc_diag[:, P * s_tile:P * s_tile + P], vt[:, tt, P * g:P * g + P], start=(g % 4 == 0),
                             stop=(tt == 0), skip_group_check=True)
                    if tt:
                        ins = MM(o, sc_cross[:, P * g:P * g + P], vt[:, 0, P * g:P * g + P], start=False, stop=True,
                                 skip_group_check=True)
                ins.then_inc(rec["o"], 1)

            pe.wait_ge(chunk_freed_v, V_FREED[E0["rec_i"] + 1])
            pe.wait_ge(chunk_freed_s, S_FREED[E0["rec_i"] + 1])
            pe.wait_ge(rec["kx"], 8)
            pe.wait_ge(rec["qx"], 8)
            for g in range(REC_H):
                ins = MM(psC[:, g // 4, P * (g % 4):P * (g % 4) + P], X[1][:, T * g:T * g + P], X[1][:, T * g + P:T * g + T],
                         start=(g % 4 == 0), stop=True, skip_group_check=True)
            ins.then_inc(rec["cross"], 1)
            pe.wait_ge(rec["picked"], 16)
            outputs(0)
            pe.wait_ge(rec["crossed"], 1)
            outputs(1)
            for tt in range(TT):
                for k in range(KT):
                    if k % 4 == 0:
                        pe.wait_ge(rec["gated"], 2 * tt + k // 4 + 1)
                    at = (k % 2) * T + tt * P
                    nc.tensor.transpose(psC[:, k // 2, at:at + P], X[1][:, tt * D + k * P:tt * D + k * P + P],
                                        ident[:, :]).then_inc(rec["turned"], 1)
            gather("rec_o", ot, rec["olo"], 2)


N_CONSTS = 2 + 1 + 6 + 1 + 7
E_FIRST = [E0[n] for n in ("sb_qk", "ffn0", "fox_k", "ffn1", "at_q", "rec_f")]
U0_END = [U0["sb_o"] + 4, U0["ffn0"] + 3 * NJ, U0["fox_o"] + 4, U0["ffn1"] + 3 * NJ, U0["at_o"] + 4, U0["rec_o"] + 4]


ROWS0 = [0, 1, 4, 5, 8, 9]


def xt_base(n):
    return 4 * n + (8 if n > 2 else 0)


def column_units(w):
    n = w.shape[1] // 512
    return np.ascontiguousarray(w.reshape(2, 4, P, n, 512).transpose(3, 0, 2, 1, 4)).reshape(2 * n, P, UNIT)


def ffn_units(up, down):
    cols = np.stack([up[:, :FF].reshape(D, NJ, 256), up[:, FF:].reshape(D, NJ, 256)], axis=2)
    ups = column_units(cols.reshape(D, NJ * 512)).reshape(NJ, 2, P, UNIT)
    downs = down.reshape(NJ, 2, P, D).transpose(0, 2, 1, 3).reshape(NJ, P, UNIT)
    order = [ups[0, 0], ups[0, 1]]
    for j in range(1, NJ - 2):
        order += [ups[j, 0], ups[j, 1], downs[j - 1]]
    order += [*ups[NJ - 2], *ups[NJ - 1], *downs[NJ - 3:]]
    return np.stack(order)


def per_partition(v):
    return v.reshape(-1, P).T


def kernel(**a):
    import concourse.bacc as bacc
    from concourse.bass_utils import run_bass_kernel_spmd

    a = {k: np.asarray(v) for k, v in a.items()}
    w_kvf, w_at, w_rec = a["w_kvf"], a["attn_w_in_2"][0], a["rec_w_in_2"][0]
    kv_cols = w_at[:, D:D + 256].reshape(KT, P, 256).transpose(1, 0, 2).reshape(1, P, UNIT)
    stream = np.concatenate([
        column_units(a["sb_w_qkv"][0]), column_units(a["sb_w_o"][0]), ffn_units(a["w_up"][0], a["w_down"][0]),
        column_units(w_kvf[:, :2 * D]), column_units(a["fox_w_q"][0]), column_units(a["fox_w_o"][0]),
        ffn_units(a["w_up"][1], a["w_down"][1]),
        column_units(w_at[:, :D]), kv_cols, column_units(w_at[:, D + 256:]), column_units(a["attn_w_out_2"][0]),
        column_units(w_rec[:, D:2 * D]), column_units(w_rec[:, :D]), column_units(w_rec[:, 3 * D:]),
        column_units(w_rec[:, 2 * D:3 * D]), column_units(a["rec_w_out_2"][0])])
    conv = np.concatenate([a["conv_w"], a["conv_b"][:, None, :]], axis=1)
    conv = conv.reshape(2, 4, 2, FF // P, P).transpose(4, 0, 3, 2, 1).reshape(P, -1)
    pvec = np.concatenate([
        per_partition(a["sb_pre_g"][0]), per_partition(a["kv_norm_g"]), per_partition(a["fox_pre_g"][0]),
        per_partition(a["ffn_pre_g"][0]), per_partition(a["ffn_pre_g"][1]), per_partition(a["pre_norm_w_2"][0]),
        per_partition(a["pre_norm_w_2"][1]), per_partition(a["attn_b_in_2"][0][D + 256:]),
        per_partition(a["rec_lb_logits_2"][0]), per_partition(a["rec_lb_logits_2"][1]), conv], axis=1)
    post_g = np.stack([a["sb_post_g"][0], a["ffn_post_g"][0], a["fox_post_g"][0], a["ffn_post_g"][1],
                       a["post_norm_w_2"][0], a["post_norm_w_2"][1]])
    arrays = {
        "stream": stream, "pvec": pvec, "post_g": post_g, "x_in": a["x"],
        "wf": w_kvf[:, 2 * D:].reshape(KT, P, H).transpose(1, 0, 2), "bf": a["b_f"].reshape(H, 1),
        "b_in": a["attn_b_in_2"][0][:D + 256], "b_out": a["attn_b_out_2"][0], "sinks": a["attn_sinks_2"][0],
        "gnorm": a["rec_gnorm_w_2"][0], "pos": a["positions_2"].reshape(TT, P).T}
    arrays = {k: np.ascontiguousarray(v) for k, v in arrays.items()}

    nc = bacc.Bacc("TRN2", target_bir_lowering=False, num_devices=1)
    args = [nc.dram_tensor(k, v.shape, mybir.dt.from_np(v.dtype), kind="ExternalInput").ap() for k, v in arrays.items()]
    out = nc.dram_tensor("out", (1, T, D), F32, kind="ExternalOutput").ap()
    build(nc, *args, out)
    r = run_bass_kernel_spmd(nc, [arrays], core_ids=[0])
    return r.results[0]["out"]
```
